# Optimizing a Trainium2 kernel written in Bass

```python
import jax, jax.numpy as jnp
from jax import lax
import numpy as np

D_MODEL = 1024
BATCH = 1
SEQ = 512
DEPTH = 2
DEC_BATCH = 1
DEC_SEQ = 64
PAST_LEN = 512

CHUNK = 64
CONV_WIDTH = 3
D_CONV = D_MODEL
N_HEADS = 8
QK_NOPE = 128
QK_ROPE = 64
QK_DIM = QK_NOPE + QK_ROPE
V_DIM = D_MODEL // N_HEADS
Q_LORA = 384
KV_LORA = 256
D_FF = 4 * D_MODEL
ROPE_THETA = 10000.0
EPS = 1e-6
Q_BLOCK = 128
SM_SCALE = QK_DIM ** -0.5
NEG_INF = -1e30

OFF_C = D_CONV
OFF_X = 2 * D_CONV
OFF_Q = 3 * D_CONV
OFF_KV = OFF_Q + Q_LORA
OFF_PE = OFF_KV + KV_LORA
OFF_GA = OFF_PE + QK_ROPE
OFF_GB = OFF_GA + D_MODEL
D_IN = OFF_GB + D_MODEL

kernel_name = "hybrid_shortconv_mla_stream_step"

def rmsnorm(x, g):
    xf = x.astype(jnp.float32)
    y = xf * lax.rsqrt(jnp.mean(xf * xf, axis=-1, keepdims=True) + EPS)
    return (y * g.astype(jnp.float32)).astype(x.dtype)

def rope_tables(pos):
    inv = ROPE_THETA ** (-jnp.arange(0, QK_ROPE, 2, dtype=jnp.float32) / QK_ROPE)
    ang = pos.astype(jnp.float32)[:, None] * inv[None, :]
    return jnp.cos(ang), jnp.sin(ang)

def apply_rope(x, cos, sin):
    if x.ndim == 4:
        cos, sin = cos[:, None, :], sin[:, None, :]
    xf = x.astype(jnp.float32)
    x1, x2 = jnp.split(xf, 2, axis=-1)
    out = jnp.concatenate([x1 * cos - x2 * sin, x2 * cos + x1 * sin], axis=-1)
    return out.astype(x.dtype)

def short_conv(u, buf, w):
    L = u.shape[1]
    full = jnp.concatenate([buf, u], axis=1)
    y = sum(w[k][None, None, :] * full[:, k:k + L] for k in range(CONV_WIDTH))
    return y, full[:, -(CONV_WIDTH - 1):]

def mla_attention(q_nope, q_pe, q_pos, ckv, kpe, k_pos, w_uk, w_uv):
    B, Lq = q_nope.shape[0], q_nope.shape[1]
    k_nope = jnp.einsum('bkc,chd->bkhd', ckv, w_uk.reshape(KV_LORA, N_HEADS, QK_NOPE))
    v = jnp.einsum('bkc,chd->bkhd', ckv, w_uv.reshape(KV_LORA, N_HEADS, V_DIM))
    k_chunk = k_pos // CHUNK
    qb = min(Q_BLOCK, Lq)
    nb = Lq // qb
    qn_b = jnp.moveaxis(q_nope.reshape(B, nb, qb, N_HEADS, QK_NOPE), 1, 0)
    qp_b = jnp.moveaxis(q_pe.reshape(B, nb, qb, N_HEADS, QK_ROPE), 1, 0)
    qpos_b = q_pos.reshape(nb, qb)

    def block(args):
        qn, qp, qpos = args
        s = (jnp.einsum('bqhd,bkhd->bhqk', qn, k_nope)
             + jnp.einsum('bqhr,bkr->bhqk', qp, kpe)).astype(jnp.float32) * SM_SCALE
        mask = k_chunk[None, :] <= (qpos // CHUNK)[:, None]
        s = jnp.where(mask[None, None], s, NEG_INF)
        p = jax.nn.softmax(s, axis=-1).astype(v.dtype)
        return jnp.einsum('bhqk,bkhd->bqhd', p, v)

    out = lax.map(block, (qn_b, qp_b, qpos_b))
    return jnp.moveaxis(out, 0, 1).reshape(B, Lq, N_HEADS * V_DIM)

def layer(x, pos, conv_buf, past_ckv, past_kpe, past_pos,
          w_in, conv_w, w_uq, w_uk, w_uv, w_o, w1, w2,
          g_pre_mix, g_post_mix, g_pre_ffn, g_post_ffn, g_q, g_kv):
    B, L, _ = x.shape
    h = rmsnorm(x, g_pre_mix)
    z = h @ w_in
    b_g, c_g, xin, cq, ckv_raw, kpe_raw, ga, gb = jnp.split(
        z, [OFF_C, OFF_X, OFF_Q, OFF_KV, OFF_PE, OFF_GA, OFF_GB], axis=-1)
    yc, new_buf = short_conv(c_g * xin, conv_buf, conv_w)
    y_a = b_g * yc
    cos, sin = rope_tables(pos)
    q = (rmsnorm(cq, g_q) @ w_uq).reshape(B, L, N_HEADS, QK_DIM)
    q_nope, q_pe = q[..., :QK_NOPE], apply_rope(q[..., QK_NOPE:], cos, sin)
    ckv_new = rmsnorm(ckv_raw, g_kv)
    kpe_new = apply_rope(kpe_raw, cos, sin)
    if past_ckv is None:
        ckv_all, kpe_all, k_pos = ckv_new, kpe_new, pos
    else:
        ckv_all = jnp.concatenate([past_ckv, ckv_new], axis=1)
        kpe_all = jnp.concatenate([past_kpe, kpe_new], axis=1)
        k_pos = jnp.concatenate([past_pos, pos])
    y_b = mla_attention(q_nope, q_pe, pos, ckv_all, kpe_all, k_pos, w_uk, w_uv)
    merged = jax.nn.sigmoid(ga) * y_a + jax.nn.sigmoid(gb) * y_b
    x = x + rmsnorm(merged @ w_o, g_post_mix)
    f = jnp.square(jax.nn.relu(rmsnorm(x, g_pre_ffn) @ w1)) @ w2
    x = x + rmsnorm(f, g_post_ffn)
    return x, new_buf, ckv_new, kpe_new

def setup_inputs(seed: int = 0) -> dict:
    key = jax.random.key(seed)
    ks = jax.random.split(key, 24)
    f32 = jnp.float32

    def nrm(k, shape, scale):
        return jax.random.normal(k, shape, f32) * scale

    def gain(k, n):
        return 1.0 + 0.05 * jax.random.normal(k, (DEPTH, n), f32)

    return {
        "x_prompt": nrm(ks[0], (BATCH, SEQ, D_MODEL), 1.0),
        "x_sample": nrm(ks[1], (DEC_BATCH, DEC_SEQ, D_MODEL), 1.0),
        "cache_ckv": nrm(ks[2], (DEPTH, DEC_BATCH, PAST_LEN, KV_LORA), 1.0),
        "cache_kpe": nrm(ks[3], (DEPTH, DEC_BATCH, PAST_LEN, QK_ROPE), 1.0),
        "state_conv": nrm(ks[4], (DEPTH, DEC_BATCH, CONV_WIDTH - 1, D_CONV), 1.0),
        "w_in": nrm(ks[5], (DEPTH, D_MODEL, D_IN), D_MODEL ** -0.5),
        "conv_w": nrm(ks[6], (DEPTH, CONV_WIDTH, D_CONV), CONV_WIDTH ** -0.5),
        "w_uq": nrm(ks[7], (DEPTH, Q_LORA, N_HEADS * QK_DIM), Q_LORA ** -0.5),
        "w_uk": nrm(ks[8], (DEPTH, KV_LORA, N_HEADS * QK_NOPE), KV_LORA ** -0.5),
        "w_uv": nrm(ks[9], (DEPTH, KV_LORA, N_HEADS * V_DIM), KV_LORA ** -0.5),
        "w_o": nrm(ks[10], (DEPTH, D_MODEL, D_MODEL), D_MODEL ** -0.5),
        "w1": nrm(ks[11], (DEPTH, D_MODEL, D_FF), D_MODEL ** -0.5),
        "w2": nrm(ks[12], (DEPTH, D_FF, D_MODEL), D_FF ** -0.5),
        "g_pre_mix": gain(ks[13], D_MODEL),
        "g_post_mix": gain(ks[14], D_MODEL),
        "g_pre_ffn": gain(ks[15], D_MODEL),
        "g_post_ffn": gain(ks[16], D_MODEL),
        "g_q": gain(ks[17], Q_LORA),
        "g_kv": gain(ks[18], KV_LORA),
    }

def reference(x_prompt, x_sample, cache_ckv, cache_kpe, state_conv,
              w_in, conv_w, w_uq, w_uk, w_uv, w_o, w1, w2,
              g_pre_mix, g_post_mix, g_pre_ffn, g_post_ffn, g_q, g_kv):
    B, S, _ = x_prompt.shape
    P = cache_ckv.shape[2]
    Ls = x_sample.shape[1]
    pos_p = jnp.arange(S, dtype=jnp.int32)
    past_pos = jnp.arange(P, dtype=jnp.int32)
    pos_s = P + jnp.arange(Ls, dtype=jnp.int32)
    zero_buf = jnp.zeros((B, CONV_WIDTH - 1, D_CONV), x_prompt.dtype)

    xp, xs = x_prompt, x_sample
    ckv_p, kpe_p, conv_p, ckv_s, kpe_s, conv_s = [], [], [], [], [], []
    for l in range(DEPTH):
        wl = (w_in[l], conv_w[l], w_uq[l], w_uk[l], w_uv[l], w_o[l], w1[l], w2[l],
              g_pre_mix[l], g_post_mix[l], g_pre_ffn[l], g_post_ffn[l], g_q[l], g_kv[l])
        xp, bp, cp, kp = layer(xp, pos_p, zero_buf, None, None, None, *wl)
        xs, bs, cs, ksm = layer(xs, pos_s, state_conv[l], cache_ckv[l], cache_kpe[l],
                                past_pos, *wl)
        ckv_p.append(cp); kpe_p.append(kp); conv_p.append(bp)
        ckv_s.append(cs); kpe_s.append(ksm); conv_s.append(bs)

    return (xp, xs,
            jnp.stack(ckv_p), jnp.stack(kpe_p), jnp.stack(conv_p),
            jnp.stack(ckv_s), jnp.stack(kpe_s), jnp.stack(conv_s))


_drawn_inputs = setup_inputs


def setup_inputs(seed=0):
    import zlib

    import numpy as np

    out = dict(_drawn_inputs(seed))
    spreads = {}
    factors = {'g_q': 8.0}
    for name, (base, spread) in spreads.items():
        noise = np.random.default_rng([zlib.crc32(name.encode()), seed]).standard_normal(out[name].shape)
        drawn = base * np.exp(spread * noise) if base else spread * noise
        out[name] = __import__('jax').numpy.asarray(drawn.astype(out[name].dtype))
    for name, factor in factors.items():
        out[name] = (out[name] * factor).astype(out[name].dtype)
    return out
```

```python
from contextlib import ExitStack

import numpy as np

import concourse.bass as bass
from concourse import mybir

F32 = mybir.dt.float32
F32R = mybir.dt.float32r
ALU = mybir.AluOpType
ACT = mybir.ActivationFunctionType
AXX = mybir.AxisListType.X

P = 128
D = 1024
DEPTH = 2
NP_, NS_ = 512, 64
NT = NP_ + NS_
NH = 288
PAST = 512
HEADS = 8
QL, KL = 384, 256
NOPE, ROPE = 128, 64
QK = NOPE + ROPE
DFF = 4 * D
CH = 64
EPS = 1e-6
SCALE = float(QK) ** -0.5
NEG = -1e30
KC = D // P
QC, CC = QL // P, KL // P
KT = NP_ // P
GROUPS = DFF // 512

N_P1, N_HEAD, N_WO, N_GRP = 6, 5, 8, 4
NB = N_P1 + N_HEAD * HEADS + N_WO + 2 * N_GRP * GROUPS
SLOT_P1 = [4, 1, 2, 3, 0, 4]
SLOT_HD = [1, 2, 3, 0, 4]
SLOT_WO = [1, 2, 3, 0, 4, 5, 6, 7]
SLOT_W1 = [1, 2, 3, 0]
SLOT_W2 = [4, 5, 6, 7]
SLOT_USES = [19, 19, 19, 19, 18, 8, 8, 8]


def n_head(h, i):
    return N_P1 + N_HEAD * h + i


def n_wo(m):
    return N_P1 + N_HEAD * HEADS + m


def n_w1(g, j):
    return n_wo(8) + j if g == 0 else n_wo(8) + 8 * g - 4 + j


def n_w2(g, j):
    return n_wo(8) + 8 + 8 * g + j if g < GROUPS - 1 else NB - 4 + j


def use_p1(b):
    return 2 if b == 5 else 1


def use_hd(h, i):
    return h + (3 if SLOT_HD[i] == 4 else 2)


def use_wo(m):
    s = SLOT_WO[m]
    return 11 if s == 4 else 10 if s < 4 else 1


def use_w1(g, j):
    return g + 11


def use_w2(g, j):
    return g + (12 if SLOT_W2[j] == 4 else 2)


RING = 184
RING0 = 2
P1_A, P1_B = [0, 1, 2, 3, 8, 12], [4, 5, 6, 7, 10, 14]
P1_SUM = [9, 11, 13, 15]
HD0 = 16


def r_hd(h, i, s):
    return HD0 + 10 * h + 2 * i + s


R3 = HD0 + 10 * HEADS
WO_A = [R3 + m for m in range(8)]
WO_SUM_A = R3 + 8
WO_B = [R3 + m for m in (9, 10, 11, 12, 13, 14, 16, 17)]
FF_SUM_A = R3 + 15
FF_A = [R3 + m for m in (18, 20, 21, 22)]
WO_SUM_B = R3 + 19
FF_SUM_B = R3 + 23
FF_B = [R3 + m for m in (24, 25, 26, 27)]


def r_w1(g, s, j):
    return (FF_A, FF_B)[s][j] if g == 0 else R3 + 28 + 8 * (g - 1) + 4 * s + j


W2N = 16 * GROUPS
END_SUM = [180, 181, 182, 183]
assert r_w1(GROUPS - 1, 1, 3) == 179

G_PRE, G_POST, G_FF, G_FPOST, G_Q, G_KV, G_CONV = 0, 8, 16, 24, 32, 35, 37
NG = 37 + 24
SWE, SWO = 1536, 1152
UQ, UK, UV, UKT, UPE = 0, 384, 640, 896, 1152
PO = [0, 128, 384, 768]
PTO = [0, 512, 896, 1152]


PCOLS = sum(P * (t + 1) for t in range(KT))
C_ID, C_ONE, C_EPS, C_GAIN = 0, P, 2 * P, 2 * P + 1
C_STATE = C_GAIN + (DEPTH + 1) * NG
N_CONST = C_STATE + DEPTH * KC * 2
OWN_1, OWN_PAIR, OWN_3, OWN_4 = 5, 30, 20, 24
OWN_L = OWN_1 + (HEADS // 2) * OWN_PAIR + OWN_3 + OWN_4


def bank(idx):
    return (RING0 + idx) % 4


class Plan:

    def __init__(self, nc, ctx):
        self.nc = nc
        self.memory()
        self.ring = ctx.enter_context(nc.psum_tensor("ring", [P, 4, 512], F32))
        self.att = ctx.enter_context(nc.psum_tensor("att", [P, 4 * 512], F32))

        def semaphore(name):
            return ctx.enter_context(nc.semaphore(name))

        self.consts_landed = semaphore("consts_landed")
        self.x_landed0 = semaphore("x_landed0")
        self.x_landed1 = semaphore("x_landed1")
        self.x_landed2 = semaphore("x_landed2")
        self.x_landed3 = semaphore("x_landed3")
        self.tables_landed = semaphore("tables_landed")
        self.small_landed = semaphore("small_landed")
        self.cache_landed = semaphore("cache_landed")
        self.nat_landed = semaphore("nat_landed")
        self.slot0 = semaphore("slot0")
        self.slot1 = semaphore("slot1")
        self.slot2 = semaphore("slot2")
        self.slot3 = semaphore("slot3")
        self.slot4 = semaphore("slot4")
        self.slot5 = semaphore("slot5")
        self.slot6 = semaphore("slot6")
        self.slot7 = semaphore("slot7")
        self.weights_hi = semaphore("weights_hi")
        self.weights_lo = semaphore("weights_lo")
        self.small_hi = semaphore("small_hi")
        self.small_lo = semaphore("small_lo")
        self.ring_full = semaphore("ring_full")
        self.ring_free = semaphore("ring_free")
        self.w2_full = semaphore("w2_full")
        self.w2_free = semaphore("w2_free")
        self.squared = semaphore("squared")
        self.summed = semaphore("summed")
        self.rooted = semaphore("rooted")
        self.x_hi = semaphore("x_hi")
        self.x_lo = semaphore("x_lo")
        self.x_new = semaphore("x_new")
        self.latent_f = semaphore("latent_f")
        self.latent_hi = semaphore("latent_hi")
        self.latent_lo = semaphore("latent_lo")
        self.rope_swapped = semaphore("rope_swapped")
        self.rope_sum = semaphore("rope_sum")
        self.rope_hi = semaphore("rope_hi")
        self.rope_lo = semaphore("rope_lo")
        self.sample_kept = semaphore("sample_kept")
        self.projected = semaphore("projected")
        self.proj_hi = semaphore("proj_hi")
        self.proj_lo = semaphore("proj_lo")
        self.absorbed = semaphore("absorbed")
        self.abs_hi = semaphore("abs_hi")
        self.abs_lo = semaphore("abs_lo")
        self.pe_sample = semaphore("pe_sample")
        self.scored = semaphore("scored")
        self.row_max = semaphore("row_max")
        self.exped = semaphore("exped")
        self.normed = semaphore("normed")
        self.turned = semaphore("turned")
        self.turned_hi = semaphore("turned_hi")
        self.turned_lo = semaphore("turned_lo")
        self.pv_made = semaphore("pv_made")
        self.pv_read = semaphore("pv_read")
        self.gated = semaphore("gated")
        self.conv_first = semaphore("conv_first")
        self.merged = semaphore("merged")
        self.cache_hi = semaphore("cache_hi")
        self.cache_lo = semaphore("cache_lo")
        self.new_turned = semaphore("new_turned")
        self.s_scored = semaphore("s_scored")
        self.s_max = semaphore("s_max")
        self.s_exped = semaphore("s_exped")
        self.s_normed = semaphore("s_normed")
        self.s_turned = semaphore("s_turned")
        self.s_thi = semaphore("s_thi")
        self.s_tlo = semaphore("s_tlo")
        self.s_context = semaphore("s_context")
        self.s_chi = semaphore("s_chi")
        self.s_clo = semaphore("s_clo")
        self.s_valued = semaphore("s_valued")
        self.s_merged = semaphore("s_merged")
        self.f_made = semaphore("f_made")
        self.f_hi = semaphore("f_hi")
        self.f_lo = semaphore("f_lo")
        self.latents_stored = semaphore("latents_stored")
        self.conv_stored = semaphore("conv_stored")
        self.x_stored = semaphore("x_stored")
        self.dve_own = semaphore("dve_own")
        self.waits_apart = semaphore("waits_apart")
        self.slots = [self.slot0, self.slot1, self.slot2, self.slot3, self.slot4, self.slot5, self.slot6, self.slot7]
        self.x_landed = [self.x_landed0, self.x_landed1, self.x_landed2, self.x_landed3]

    def memory(self):
        start = (self.nc.sbuf_base + 31) // 32 * 32
        top = self.nc.sbuf_usable_end
        mark = [start]

        def put(name, shape, dt=F32):
            size = (4 * int(np.prod(shape[1:])) + 31) // 32 * 32
            at = mark[0]
            mark[0] = at + size
            assert mark[0] <= top, f"{name} ends {mark[0] - top} bytes past the end"
            return self.nc.alloc_sbuf_tensor_at(name, shape, dt, offset=at)

        def split(name, shape, raw=False):
            hi = put(name + "_hi", shape, F32R)
            at = mark[0]
            lo = put(name + "_lo", shape, F32R)
            if not raw:
                return hi, lo
            return hi, lo, self.nc.alloc_sbuf_tensor_at(name + "_raw", shape, F32, offset=at)

        self.x = put("x", [P, KC, NT])
        self.consts = put("consts", [P, N_CONST])
        self.rx, self.rx2 = put("rx", [P, NT]), put("rx2", [P, NT])
        self.conv_tail = put("conv_tail", [P, KC, 4])
        self.kv_sample = put("kv_sample", [P, CC, NS_])
        self.xh, self.xl = split("xs", [P, KC, NT])
        self.my = put("my", [P, KC, NT])
        self.sh, self.sl, self.sraw = split("small", [P, SWE], raw=True)
        self.wh, self.wl, self.wraw = split("w", [P, 5, 1024], raw=True)
        self.qah, self.qal = split("q_abs", [P, CC, HEADS * NS_])
        self.qph, self.qpl = split("q_pe_sample", [ROPE, HEADS * NS_])
        self.sgb = put("gate_sample", [P, KC, NS_])
        tables = mark[0]
        self.cos, self.sin = put("cos", [P, NT]), put("sin", [P, NT])
        shared = mark[0]
        mark[0] = tables
        self.ss, self.sq = put("ss", [P, 2, NH]), put("sq", [P, 2, NH])
        mark[0] = shared
        self.cqh, self.cql = split("cqn", [P, QC, NT])
        self.kvh, self.kvl = split("ckv", [P, CC, NT])
        self.keh, self.kel = split("kpe", [P, NT])
        after_latents = mark[0]
        self.qh, self.ql = split("q", [P, NT])
        self.peh, self.pel = split("q_pe", [P, NT])
        self.kh, self.kl = split("k", [P, NP_])
        self.vh, self.vl = split("v", [P, NP_])
        probs = mark[0]
        self.probs = put("probs", [P, PCOLS])
        self.pth, self.ptl = split("probs_t", [P, PCOLS])
        self.mx, self.nmx = put("mx", [P, KT]), put("nmx", [P, KT])
        self.rs, self.ri = put("rs", [P, KT]), put("ri", [P, KT])
        self.gb, self.ga = put("gb", [P, NT]), put("ga", [P, NT])
        self.cv = put("cv", [P, NT + 2])
        self.u = put("u", [P, NT + 4])
        self.ybt = put("ybt", [P, NP_])
        rope = mark[0]
        self.bt = put("bt", [P, NT])
        mark[0] = rope
        self.rope_t, self.rope_s = put("rope_t", [P, NH]), put("rope_s", [P, NH])
        mark[0] = after_latents
        self.cq = put("cq", [P, QC, NT])
        self.rk = put("rk", [P, 2, NT])
        self.ss1 = put("ss1", [P, 4, NH])
        assert mark[0] <= probs
        mark[0] = probs
        self.kv = put("kv", [P, CC, NT])
        self.kpe = put("kpe", [P, NT])
        self.sq1 = put("sq1", [P, 2, NH])
        self.rope1_t, self.rope1_s = put("rope1_t", [P, NH]), put("rope1_s", [P, NH])
        assert mark[0] <= probs + 3 * 4 * PCOLS
        mark[0] = shared
        self.cth, self.ctl, self.ctraw = split("cache_t", [P, CC, PAST], raw=True)
        self.kch, self.kcl, self.kcraw = split("cache_pe", [ROPE, PAST], raw=True)
        assert mark[0] <= shared + 2 * 4 * QC * NT
        mark[0] = after_latents
        self.nah, self.nal, self.naraw = split("cache_n", [P, 5, KL], raw=True)
        self.ps = put("probs_s", [P, NT])
        self.tsh, self.tsl = split("probs_s_t", [P, 5, P])
        self.och, self.ocl = split("context_s", [P, CC, P])
        self.ys = put("y_s", [P, 2, NS_])
        self.stat = put("stat_s", [P, 4])
        sample_end = mark[0]
        mark[0] = (top - 2 * 3 * 4096) // 32 * 32
        slots = mark[0]
        assert sample_end <= slots
        self.w8h, self.w8l, self.w8raw = split("w8", [P, 3, 1024], raw=True)
        mark[0] = shared
        self.fh, self.fl = split("f", [P, 2, 4, NT])
        self.ft, self.ff = put("ft", [P, 2, NH]), put("ff", [P, 2, NH])
        assert mark[0] <= slots

    def slot(self, s):
        if s < 5:
            return self.wh[:, s, :], self.wl[:, s, :], self.wraw[:, s, :]
        return self.w8h[:, s - 5, :], self.w8l[:, s - 5, :], self.w8raw[:, s - 5, :]

    def const(self, c, n=1):
        return self.consts[:, c:c + n]

    def gain(self, L, c, ahead=0):
        return self.consts[:, bass.ds(L * NG + (C_GAIN + ahead * NG + c), 1)]


def full(L, idx):
    return L * RING + (RING + RING0 + idx + 1)


def may_fill(L, idx):
    return L * RING + (RING0 + idx + 1)


def freed(L, idx):
    return L * RING + (RING0 + idx + 5)


def w2_filled(L, g, k):
    return L * W2N + (W2N + 16 * g + k + 1)


def w2_may_fill(L, g, k):
    return L * W2N + (16 * g + k + 1)


def x_part(L, i):
    return L * 52 + (8 + i + 1)


X_WOA, X_WOB, X_WOS, X_FFA, X_FFB, X_NXA, X_NXB = 0, 8, 16, 20, 28, 36, 44


def square(L, i):
    return L * 74 + (16 + i + 1)


S_CQA, S_KVA0, S_CQB, S_KVB0, S_KVA1, S_KVB1 = 0, 3, 4, 7, 8, 9
S_POSTA, S_PREA, S_POSTB, S_PREB, S_FPA, S_MIX, S_NXB = 10, 18, 26, 34, 42, 50, 66


def root(L, e):
    return L * 12 + (2 + e + 1)


def cols(s):
    return slice(NH * s, NH * (s + 1))


def mm3(pe, out, w, x, first, last):
    pe.matmul(out, w[1], x[0], start=first, stop=False)
    pe.matmul(out, w[0], x[1], start=False, stop=False)
    return pe.matmul(out, w[0], x[0], start=False, stop=last)


class Own:

    def __init__(self, dve, sem, base, steps):
        self.dve, self.sem, self.base, self.steps, self.n = dve, sem, base, steps, 0

    def step(self, ins):
        ins.then_inc(self.sem, 1)
        self.n += 1

    def wait(self, back=0):
        self.dve.wait_ge(self.sem, self.base + (self.n - back))

    def done(self):
        assert self.n == self.steps, (self.n, self.steps)


def program(nc, x_in, consts, tables, blocks, small, uv, cache_t, cache_n, cache_pe,
            x_out, kv_out, kpe_out, conv_out):
    with ExitStack() as ctx:
        pl = Plan(nc, ctx)
        block = ctx.enter_context(nc.Block())
        loads(nc, block, pl, x_in, consts, tables, blocks, small, uv, cache_t, cache_n, cache_pe, x_out)
        sums(nc, block, pl)
        scalar_engine(nc, block, pl, kv_out, kpe_out, conv_out)
        vector_engine(nc, block, pl)
        tensor_engine(nc, block, pl)


def loads(nc, block, pl, x_in, consts, tables, blocks, small, uv, cache_t, cache_n, cache_pe, x_out):

    @block.sync
    def _(sp):
        def slot_load(L, n, s):
            sp.dma_start(pl.slot(s)[2], blocks[L * NB + n]).then_inc(pl.slots[s], 16)

        sp.dma_start(pl.consts[:, :], consts).then_inc(pl.consts_landed, 16)
        for i in range(4):
            sp.dma_start(pl.x[:, 2 * i:2 * i + 2, :], x_in[:, 2 * i:2 * i + 2, :]).then_inc(pl.x_landed[i], 16)

        with sp.Fori(0, DEPTH) as L:
            sp.wait_ge(pl.w2_full, L * W2N + 16 * (GROUPS - 2) + 9 + 1)
            slot_load(L, 0, SLOT_P1[0])
            for j in range(4):
                sp.wait_ge(pl.w2_full, L * W2N + 16 * (GROUPS - 1) + 8 + 2 * j + 1 + 1)
                slot_load(L, 1 + j, SLOT_P1[1 + j])
            sp.wait_ge(pl.s_valued, L * 4 + 1)
            sp.dma_start(pl.sraw[:, :], small[L * 5][:, 0:SWE]).then_inc(pl.small_landed, 16)
            sp.wait_ge(pl.ring_free, freed(L, -1))
            sp.dma_start(pl.cos[:, :], tables[0]).then_inc(pl.tables_landed, 16)
            sp.dma_start(pl.sin[:, :], tables[1]).then_inc(pl.tables_landed, 16)
            sp.wait_ge(pl.ring_full, full(L, P1_B[0]))
            slot_load(L, 5, SLOT_P1[5])
            for i in range(N_HEAD):
                sp.wait_ge(pl.ring_full, full(L, P1_B[1 + i]))
                slot_load(L, n_head(0, i), SLOT_HD[i])
            with sp.Fori(0, HEADS // 2) as p:
                for e in range(2):
                    for i in range(N_HEAD):
                        if i == 2:
                            sp.wait_ge(pl.absorbed, L * HEADS + p * 2 + (e + 1))
                            if e == 0:
                                sp.dma_start(pl.sraw[:, 0:SWO], small[L * 5 + p][:, SWE:SWE + SWO]) \
                                    .then_inc(pl.small_landed, 16)
                            else:
                                sp.dma_start(pl.sraw[:, :], small[L * 5 + (p + 1)][:, 0:SWE]) \
                                    .then_inc(pl.small_landed, 16)
                        sp.wait_ge(pl.ring_full, L * RING + p * 20 + (RING + RING0 + r_hd(e, i, 1) + 1))
                        sp.dma_start(pl.slot(SLOT_HD[i])[2], blocks[L * NB + p * 10 + (n_head(e + 1, i))]) \
                            .then_inc(pl.slots[SLOT_HD[i]], 16)
            sp.wait_ge(pl.projected, L * 40 + 40)
            sp.dma_start(pl.ctraw[:, :, :], cache_t[L]).then_inc(pl.cache_landed, 16)
            sp.dma_start(pl.kcraw[:, :], cache_pe[L]).then_inc(pl.cache_landed, 16)
            sp.wait_ge(pl.pv_made, L * HEADS + HEADS)
            sp.dma_start(pl.naraw[:, 0:4, :], cache_n[L]).then_inc(pl.nat_landed, 16)
            sp.wait_ge(pl.merged, L * HEADS + HEADS)
            for m in range(5, 8):
                slot_load(L, n_wo(m), SLOT_WO[m])
            sp.wait_ge(pl.s_valued, L * 4 + 3)
            sp.dma_start(pl.sraw[:, 0:1024], uv[L]).then_inc(pl.small_landed, 16)
            for j in range(4):
                sp.wait_ge(pl.ring_full, full(L, WO_B[SLOT_WO.index(SLOT_W1[j])]))
                slot_load(L, n_w1(0, j), SLOT_W1[j])
            for j in range(4):
                sp.wait_ge(pl.ring_full, full(L, r_w1(0, 1, j)))
                slot_load(L, n_w1(1, j), SLOT_W1[j])
            for j in range(4):
                slot_load(L, n_w2(0, j), SLOT_W2[j])
            with sp.Fori(0, GROUPS - 2) as g:
                for j in range(4):
                    sp.wait_ge(pl.ring_full, L * RING + g * 8 + (RING + RING0 + r_w1(1, 1, j) + 1))
                    sp.dma_start(pl.slot(SLOT_W1[j])[2], blocks[L * NB + g * 8 + n_w1(2, j)]) \
                        .then_inc(pl.slots[SLOT_W1[j]], 16)
                for j in range(4):
                    sp.wait_ge(pl.w2_full, L * W2N + g * 16 + (W2N + 8 + 2 * j + 1 + 1))
                    sp.dma_start(pl.slot(SLOT_W2[j])[2], blocks[L * NB + g * 8 + n_w2(1, j)]) \
                        .then_inc(pl.slots[SLOT_W2[j]], 16)
            for j in range(4):
                sp.wait_ge(pl.ring_full, full(L, r_w1(GROUPS - 1, 1, j)))
                slot_load(L, n_w2(GROUPS - 1, j), SLOT_W1[j])
        sp.wait_ge(pl.x_new, 32 * DEPTH)
        sp.dma_start(x_out, pl.x[:, :, :]).then_inc(pl.x_stored, 16)
        sp.wait_ge(pl.x_stored, 16)


def sums(nc, block, pl):

    @block.gpsimd
    def _(pool):
        pool.sem_inc(pl.ring_full, RING)
        pool.sem_inc(pl.w2_full, W2N)
        pool.sem_inc(pl.ring_free, 4)
        pool.sem_inc(pl.w2_free, 4)
        pool.sem_inc(pl.summed, 2)
        pool.sem_inc(pl.s_valued, 1)
        pool.sem_inc(pl.pv_read, 1)

        def add(value, k, ss, sq, first):
            pool.wait_ge(pl.squared, value)
            pool.wait_ge(pl.summed, value + 1)
            if first:
                pool.sem_inc(pl.waits_apart, 1)
                nc.gpsimd.tensor_copy(ss, sq[:, k % 2, :]).then_inc(pl.summed, 1)
            else:
                nc.gpsimd.tensor_tensor(ss, ss, sq[:, k % 2, :], ALU.add).then_inc(pl.summed, 1)

        for k in range(16):
            add(k + 1, k, pl.ss[:, k % 2, :], pl.sq, k < 2)
        with pool.Fori(0, DEPTH) as L:
            for k, part, first in ((0, 0, True), (1, 0, False), (2, 0, False), (3, 2, True),
                                   (4, 1, True), (5, 1, False), (6, 1, False), (7, 3, True),
                                   (8, 2, False), (9, 3, False)):
                add(square(L, k), k, pl.ss1[:, part, :], pl.sq1, first)
            for at, half in ((S_POSTA, 0), (S_PREA, 0), (S_POSTB, 1), (S_PREB, 1), (S_FPA, 0)):
                for k in range(at, at + KC):
                    add(square(L, k), k, pl.ss[:, half, :], pl.sq, k == at)
            for m in range(KC):
                add(square(L, S_MIX + 2 * m), 0, pl.ss[:, 0, :], pl.sq, m == 0)
                add(square(L, S_MIX + 2 * m + 1), 1, pl.ss[:, 1, :], pl.sq, m == 0)
            for k in range(S_NXB, S_NXB + KC):
                add(square(L, k), k, pl.ss[:, 1, :], pl.sq, k == S_NXB)


def scalar_engine(nc, block, pl, kv_out, kpe_out, conv_out):
    act = nc.scalar

    @block.scalar
    def _(eng):
        def weight_hi(L, n, s, use):
            eng.wait_ge(pl.slots[s], (L * SLOT_USES[s] + use) * 16)
            hi, _, raw = pl.slot(s)
            act.activation(hi, raw, ACT.Copy).then_inc(pl.weights_hi, 1)

        def small_hi(L, j, n, more=0):
            eng.wait_ge(pl.small_landed, (L * 10 + (j + 1) + more) * 16)
            act.activation(pl.sh[:, 0:n], pl.sraw[:, 0:n], ACT.Copy).then_inc(pl.small_hi, 1)

        def square_of(src, L, k, sq):
            eng.wait_ge(pl.summed, square(L, k))
            act.activation(sq[:, k % 2, :], src, ACT.Square).then_inc(pl.squared, 1)

        def rooted(dst, L, idx, width):
            eng.wait_ge(pl.ring_full, full(L, idx))
            act.activation(dst, pl.ring[:, bank(idx), 0:NH], ACT.Sqrt, scale=1.0 / width,
                           bias=pl.const(C_EPS)).then_inc(pl.rooted, 1)

        def next_norm(L, m, half, col, x_new, part, k):
            cs = cols(half)
            eng.wait_ge(pl.x_new, x_new)
            apart()
            act.activation(pl.xh[:, m, cs], pl.x[:, m, cs], ACT.Copy, scale=col).then_inc(pl.x_hi, 1)
            square_of(pl.x[:, m, cs], L, k, pl.sq)

        def apart():
            eng.sem_inc(pl.waits_apart, 1)

        def rope_halves(src, s_):
            for q in range(4):
                o = q ^ 1
                ins = act.activation(s_[32 * o:32 * o + 32, :], src[32 * q:32 * q + 32, :], ACT.Copy)
            ins.then_inc(pl.rope_swapped, 1)

        eng.wait_ge(pl.consts_landed, 16)
        for m in range(KC):
            if m % 2 == 0:
                eng.wait_ge(pl.x_landed[m // 2], 16)
            act.activation(pl.xh[:, m, :], pl.x[:, m, :], ACT.Copy, scale=pl.const(C_GAIN + G_PRE + m)) \
                .then_inc(pl.x_hi, 1)
            for half in range(2):
                eng.wait_ge(pl.summed, 2 * m + half + 1)
                act.activation(pl.sq[:, half, :], pl.x[:, m, cols(half)], ACT.Square).then_inc(pl.squared, 1)
        for half in range(2):
            eng.wait_ge(pl.ring_full, RING + half + 1)
            act.activation(pl.rx[:, cols(half)], pl.ring[:, half, 0:NH], ACT.Sqrt, scale=1.0 / D,
                           bias=pl.const(C_EPS)).then_inc(pl.rooted, 1)

        with eng.Fori(0, DEPTH) as L:
            def latent_square(b, half, k):
                eng.wait_ge(pl.ring_free, freed(L, (P1_A, P1_B)[half][b]))
                src = pl.cq[:, b, cols(half)] if b < 3 else pl.kv[:, b - 3, cols(half)]
                square_of(src, L, k, pl.sq1)

            for b in range(4):
                weight_hi(L, b, SLOT_P1[b], use_p1(b))
            latent_square(0, 0, 0)
            weight_hi(L, 4, SLOT_P1[4], use_p1(4))
            for b in range(1, 4):
                latent_square(b, 0, b)
            latent_square(0, 1, 4)
            latent_square(1, 1, 5)
            weight_hi(L, 5, SLOT_P1[5], use_p1(5))
            latent_square(2, 1, 6)
            weight_hi(L, n_head(0, 0), SLOT_HD[0], use_hd(0, 0))
            latent_square(3, 1, 7)
            weight_hi(L, n_head(0, 1), SLOT_HD[1], use_hd(0, 1))
            latent_square(4, 0, 8)
            weight_hi(L, n_head(0, 2), SLOT_HD[2], use_hd(0, 2))
            small_hi(L, 0, SWE)
            rooted(pl.rk[:, 0, cols(0)], L, P1_SUM[0], QL)
            latent_square(4, 1, 9)
            rooted(pl.rk[:, 0, cols(1)], L, P1_SUM[1], QL)
            for b in range(QC):
                eng.wait_ge(pl.latent_f, L * 5 + b + 1)
                act.activation(pl.cqh[:, b, :], pl.cq[:, b, :], ACT.Copy).then_inc(pl.latent_hi, 1)
            eng.wait_ge(pl.tables_landed, L * 32 + 32)
            for half in range(2):
                eng.wait_ge(pl.ring_full, full(L, (P1_A, P1_B)[half][5]))
                rope_halves(pl.ring[:, bank((P1_A, P1_B)[half][5]), 0:NH], pl.rope1_s)
                rooted(pl.rk[:, 1, cols(half)], L, P1_SUM[2 + half], KL)
                eng.wait_ge(pl.rope_sum, L * 10 + half + 1)
                act.activation(pl.keh[:, cols(half)], pl.kpe[:, cols(half)], ACT.Copy).then_inc(pl.rope_hi, 1)
                if half == 0:
                    weight_hi(L, n_head(0, 3), SLOT_HD[3], use_hd(0, 3))
            eng.dma_start(kpe_out[L], pl.kpe[0:ROPE, :]).then_inc(pl.latents_stored, 16)
            for c in range(CC):
                eng.wait_ge(pl.latent_f, L * 5 + QC + c + 1)
                act.activation(pl.kvh[:, c, :], pl.kv[:, c, :], ACT.Copy).then_inc(pl.latent_hi, 1)
            act.activation(pl.kv_sample[:, :, :], pl.kv[:, :, NP_:NT], ACT.Copy).then_inc(pl.sample_kept, 1)
            eng.dma_start(kv_out[L], pl.kv[:, :, :]).then_inc(pl.latents_stored, 16)

            with eng.Fori(0, HEADS // 2) as p:
                for e in range(2):
                    def of_head(per_head, j):
                        return L * (HEADS * per_head) + p * (2 * per_head) + (e * per_head + j + 1)

                    def ring_freed(i, half):
                        return L * RING + p * 20 + (RING0 + r_hd(e, i, half) + 5)

                    def next_weight(i):
                        h, i2 = (e, 4) if i == 0 else (e + 1, i - 1)
                        s = SLOT_HD[i2]
                        eng.wait_ge(pl.slots[s], L * (16 * SLOT_USES[s]) + p * 32 + 16 * use_hd(h, i2))
                        hi, _, raw = pl.slot(s)
                        act.activation(hi, raw, ACT.Copy).then_inc(pl.weights_hi, 1)

                    def projected(j):
                        eng.wait_ge(pl.projected, L * 40 + p * 10 + (6 * e + j + 1))

                    eng.wait_ge(pl.ring_free, ring_freed(0, 1))
                    act.activation(pl.gb[:, :], pl.gb[:, :], ACT.Tanh, scale=0.5).then_inc(pl.gated, 1)
                    next_weight(0)
                    projected(0)
                    act.activation(pl.kh[:, :], pl.att[:, 1024:1536], ACT.Copy).then_inc(pl.proj_hi, 1)
                    projected(1)
                    act.activation(pl.vh[:, :], pl.att[:, 1536:2048], ACT.Copy).then_inc(pl.proj_hi, 1)
                    for half in range(2):
                        projected(2 + half)
                        act.activation(pl.qh[:, cols(half)], pl.att[:, 512 * half:512 * half + NH], ACT.Copy) \
                            .then_inc(pl.proj_hi, 1)
                    if e == 0:
                        for half in range(2):
                            projected(4 + half)
                            if half == 1:
                                eng.wait_ge(pl.rope_sum, L * 10 + p * 2 + 3)
                            rope_halves(pl.att[:, 512 * half:512 * half + NH], pl.rope_s)
                            eng.wait_ge(pl.rope_sum, L * 10 + p * 2 + (2 + half + 1))
                            act.activation(pl.peh[:, cols(half)], pl.rope_t[:, :], ACT.Copy).then_inc(pl.rope_hi, 1)
                        eng.wait_ge(pl.rope_lo, L * 10 + p * 2 + 4)
                        apart()
                        for hh in range(2):
                            rows = slice(64 * hh, 64 * hh + 64)
                            to = bass.ds(p * 128 + 64 * hh, 64)
                            act.activation(pl.qph[:, to], pl.peh[rows, NP_:NT].bitcast(F32), ACT.Copy) \
                                .then_inc(pl.pe_sample, 1)
                            act.activation(pl.qpl[:, to], pl.pel[rows, NP_:NT].bitcast(F32), ACT.Copy) \
                                .then_inc(pl.pe_sample, 1)
                    eng.wait_ge(pl.ring_free, ring_freed(1, 1))
                    act.activation(pl.ga[:, :], pl.ga[:, :], ACT.Tanh, scale=0.5).then_inc(pl.gated, 1)
                    next_weight(1)
                    eng.wait_ge(pl.absorbed, of_head(1, 0))
                    apart()
                    to = bass.ds(p * 128 + 64 * e, 64)
                    act.activation(pl.qah[:, :, to], pl.att[:, 1536:1664].rearrange("p (c q) -> p c q", c=2),
                                   ACT.Copy).then_inc(pl.abs_hi, 1)
                    if e == 0:
                        eng.wait_ge(pl.latents_stored, L * 32 + 32)
                    eng.wait_ge(pl.row_max, of_head(1, 0))
                    for t in range(KT):
                        act.activation(pl.probs[:, PO[t]:PO[t] + P * (t + 1)], score_tile(pl, t), ACT.Exp,
                                       scale=SCALE, bias=pl.nmx[:, t:t + 1], accum_out=pl.rs[:, t:t + 1]) \
                            .then_inc(pl.exped, 1)
                    next_weight(2)
                    eng.wait_ge(pl.small_landed, L * 160 + p * 32 + 16 * (e + 2))
                    n = SWO if e == 0 else SWE
                    act.activation(pl.sh[:, 0:n], pl.sraw[:, 0:n], ACT.Copy).then_inc(pl.small_hi, 1)
                    for k, (src, at, n) in enumerate(TURNED):
                        eng.wait_ge(pl.turned, of_head(3, k))
                        act.activation(pl.pth[:, at:at + n], pl.att[:, src:src + n], ACT.Copy) \
                            .then_inc(pl.turned_hi, 1)
                    eng.wait_ge(pl.ring_free, ring_freed(3, 1))
                    apart()
                    tail = pl.u[:, NP_:NP_ + 2 + 66].rearrange("p (a b) -> p a b", b=2)[:, 0:34:33, :]
                    act.activation(pl.conv_tail[:, p * 2 + e, :].rearrange("p (a b) -> p a b", b=2), tail, ACT.Copy)
                    act.activation(pl.cv[:, :], pl.u[:, 0:NT + 2], ACT.Copy,
                                   scale=conv_weight(pl, L, p, e, 0)).then_inc(pl.conv_first, 1)
                    next_weight(3)
                    eng.wait_ge(pl.ring_free, ring_freed(4, 1))
                    next_weight(4)

            def x_hi_a(k):
                eng.wait_ge(pl.merged, L * HEADS + k + 1)
                act.activation(pl.xh[:, k, cols(0)], pl.my[:, k, cols(0)], ACT.Copy, scale=0.5).then_inc(pl.x_hi, 1)

            weight_hi(L, n_wo(4), SLOT_WO[4], use_wo(4))
            for k in range(HEADS):
                x_hi_a(k)
            eng.dma_start(conv_out[L], pl.conv_tail[:, :, :]).then_inc(pl.conv_stored, 16)
            eng.wait_ge(pl.cache_landed, L * 32 + 32)
            act.activation(pl.cth[:, :, :], pl.ctraw[:, :, :], ACT.Copy).then_inc(pl.cache_hi, 1)
            act.activation(pl.kch[:, :], pl.kcraw[:, :], ACT.Copy).then_inc(pl.cache_hi, 1)
            eng.wait_ge(pl.nat_landed, L * 16 + 16)
            act.activation(pl.nah[:, 0:4, :], pl.naraw[:, 0:4, :], ACT.Copy).then_inc(pl.cache_hi, 1)
            eng.wait_ge(pl.new_turned, L + 1)
            act.activation(pl.nah[0:NS_, 4, :], pl.att[0:NS_, 1536:1792], ACT.Copy).then_inc(pl.cache_hi, 1)
            for k in range(HEADS):
                act.activation(pl.xh[:, k, NH:NP_], pl.my[:, k, NH:NP_], ACT.Copy, scale=0.5).then_inc(pl.x_hi, 1)

            def s_exp(t):
                eng.wait_ge(pl.s_max, L * 4 + t + 1)
                act.activation(pl.ps[:, :], pl.att[:, 0:NT], ACT.Exp, scale=SCALE, bias=pl.stat[:, 1:2],
                               accum_out=pl.stat[:, 2:3]).then_inc(pl.s_exped, 1)

            def s_turned_hi(t):
                eng.wait_ge(pl.s_turned, L * 4 + t + 1)
                act.activation(pl.tsh[:, 0:4, :], pl.att[:, 1024:1536].rearrange("p (k q) -> p k q", k=4), ACT.Copy)
                act.activation(pl.tsh[0:NS_, 4, :], pl.att[0:NS_, 576:704], ACT.Copy).then_inc(pl.s_thi, 1)

            def s_context_hi(t):
                eng.wait_ge(pl.s_context, L * 4 + t + 1)
                act.activation(pl.och[:, :, :], pl.att[:, 1664:1920].rearrange("p (c q) -> p c q", c=2), ACT.Copy) \
                    .then_inc(pl.s_chi, 1)

            def s_merged_hi(t):
                eng.wait_ge(pl.s_merged, L * 4 + t + 1)
                act.activation(pl.xh[:, 2 * t:2 * t + 2, NP_:NT], pl.my[:, 2 * t:2 * t + 2, NP_:NT], ACT.Copy,
                               scale=0.5).then_inc(pl.x_hi, 1)

            def post_square(ring_idx, m, half, k):
                eng.wait_ge(pl.ring_free, freed(L, ring_idx))
                square_of(pl.my[:, m, cols(half)], L, k, pl.sq)

            s_exp(0)
            for m in range(4):
                post_square(WO_A[m], m, 0, S_POSTA + m)
            s_turned_hi(0)
            for t in (1, 2):
                for m in (0, 1):
                    if (t, m) != (2, 1):
                        weight_hi(L, n_wo(3 + 2 * t + m), 3 + 2 * t + m, use_wo(3 + 2 * t + m))
                    post_square(WO_A[2 * t + 2 + m], 2 * t + 2 + m, 0, S_POSTA + 2 * t + 2 + m)
                    if m == 0:
                        s_context_hi(t - 1)
                        s_exp(t)
                s_merged_hi(t - 1)
                s_turned_hi(t)
            s_context_hi(2)
            small_hi(L, 9, 1024)
            s_exp(3)
            rooted(pl.rx2[:, cols(0)], L, WO_SUM_A, D)
            s_merged_hi(2)
            s_turned_hi(3)
            s_context_hi(3)
            s_merged_hi(3)
            for m in range(KC):
                next_norm(L, m, 0, pl.gain(L, G_FF + m), L * 32 + m + 1, X_FFA + m, S_PREA + m)
            for m in range(4):
                post_square(WO_B[m], m, 1, S_POSTB + m)
            for m, j in ((4, 0), (5, 1)):
                post_square(WO_B[m], m, 1, S_POSTB + m)
                weight_hi(L, n_w1(0, j), SLOT_W1[j], use_w1(0, j))
            rooted(pl.rx[:, cols(0)], L, FF_SUM_A, D)
            for m, j in ((6, 2), (7, 3)):
                post_square(WO_B[m], m, 1, S_POSTB + m)
                weight_hi(L, n_w1(0, j), SLOT_W1[j], use_w1(0, j))

            def f_hi(ready, parity, half, j):
                eng.wait_ge(pl.f_made, ready)
                act.activation(pl.fh[:, parity, j, cols(half)], pl.ff[:, j % 2, :], ACT.Copy).then_inc(pl.f_hi, 1)

            def f_ready(g, k):
                return L * 64 + (8 * g + k + 1)

            f_hi(f_ready(0, 0), 0, 0, 0)
            rooted(pl.rx2[:, cols(1)], L, WO_SUM_B, D)
            for m in range(KC):
                next_norm(L, m, 1, pl.gain(L, G_FF + m), L * 32 + 8 + m + 1, X_FFB + m, S_PREB + m)
            for j in range(1, 4):
                f_hi(f_ready(0, j), 0, 0, j)
            rooted(pl.rx[:, cols(1)], L, FF_SUM_B, D)
            for j in range(4):
                f_hi(f_ready(0, 4 + j), 0, 1, j)
                if j >= 2:
                    weight_hi(L, n_w1(1, j - 2), SLOT_W1[j - 2], use_w1(1, j - 2))
            for k in range(8):
                f_hi(f_ready(1, k), 1, k // 4, k % 4)
                if k < 2:
                    weight_hi(L, n_w1(1, k + 2), SLOT_W1[k + 2], use_w1(1, k + 2))
                elif k < 6:
                    weight_hi(L, n_w2(0, k - 2), SLOT_W2[k - 2], use_w2(0, k - 2))

            def group_weight(g, j, which):
                s = (SLOT_W1, SLOT_W2)[which][j]
                use = (use_w1(2, j), use_w2(1, j))[which]
                eng.wait_ge(pl.slots[s], L * (16 * SLOT_USES[s]) + g * 16 + 16 * use)
                hi, _, raw = pl.slot(s)
                act.activation(hi, raw, ACT.Copy).then_inc(pl.weights_hi, 1)

            eng.wait_ge(pl.conv_stored, L * 16 + 16)
            for j in range(4):
                weight_hi(L, n_w1(2, j), SLOT_W1[j], use_w1(2, j))
            with eng.Fori(0, (GROUPS - 2) // 2) as i:
                for e in range(2):
                    for k in range(8):
                        f_hi(L * 64 + i * 16 + (8 * e + 16 + k + 1), e, k // 4, k % 4)
                        if k % 2 == 1:
                            group_weight(i * 2 + e, k // 2, 1)
                    for j in range(4):
                        group_weight(i * 2 + (e + 1), j, 0)
            for m in range(KC):
                eng.wait_ge(pl.w2_free, L * W2N + 16 * (GROUPS - 1) + m + 1 + 4)
                square_of(pl.my[:, m, cols(0)], L, S_FPA + m, pl.sq)
            rooted(pl.rx2[:, cols(0)], L, END_SUM[0], D)
            for m in range(KC):
                next_norm(L, m, 0, pl.gain(L, G_PRE + m, 1), L * 32 + 16 + m + 1, X_NXA + m, S_MIX + 2 * m)
                eng.wait_ge(pl.w2_free, L * W2N + 16 * (GROUPS - 1) + 8 + m + 1 + 4)
                square_of(pl.my[:, m, cols(1)], L, S_MIX + 2 * m + 1, pl.sq)
            rooted(pl.rx[:, cols(0)], L, END_SUM[1], D)
            rooted(pl.rx2[:, cols(1)], L, END_SUM[2], D)
            for m in range(KC):
                next_norm(L, m, 1, pl.gain(L, G_PRE + m, 1), L * 32 + 24 + m + 1, X_NXB + m, S_NXB + m)
            rooted(pl.rx[:, cols(1)], L, END_SUM[3], D)
        eng.wait_ge(pl.latents_stored, 32 * DEPTH)
        eng.wait_ge(pl.conv_stored, 16 * DEPTH)


TURNED = ((1536, PTO[0], 512), (0, PTO[1], 384), (512, PTO[2], 384))


def score_tile(pl, t, width=None):
    at = (0, 128, 512, 1024)[t]
    return pl.att[:, at:at + P * (t + 1)]


def conv_weight(pl, L, p, e, tap):
    return pl.consts[:, bass.ds(L * NG + p * 6 + (C_GAIN + G_CONV + 3 * e + tap), 1)]


def vector_engine(nc, block, pl):
    dve = nc.vector

    @block.vector
    def _(eng):
        def minus(out, a, hi):
            return dve.tensor_tensor(out, a, hi.bitcast(F32), ALU.subtract)

        def weight_lo(L, n, s):
            eng.wait_ge(pl.weights_hi, L * NB + (n + 1))
            hi, lo, raw = pl.slot(s)
            minus(lo, raw, hi).then_inc(pl.weights_lo, 1)

        def small_lo(L, j, n):
            eng.wait_ge(pl.small_hi, L * 10 + (j + 1))
            minus(pl.sl[:, 0:n], pl.sraw[:, 0:n], pl.sh[:, 0:n]).then_inc(pl.small_lo, 1)

        def inverted(dst, L, idx, e):
            eng.wait_ge(pl.rooted, root(L, e))
            dve.reciprocal(dst, dst).then_inc(pl.ring_free, 1)

        for m in range(KC):
            eng.wait_ge(pl.x_hi, m + 1)
            dve.scalar_tensor_tensor(out=pl.xl[:, m, :], in0=pl.x[:, m, :], scalar=pl.const(C_GAIN + G_PRE + m),
                                     in1=pl.xh[:, m, :].bitcast(F32), op0=ALU.mult, op1=ALU.subtract) \
                .then_inc(pl.x_lo, 1)
        for half in range(2):
            eng.wait_ge(pl.rooted, half + 1)
            dve.reciprocal(pl.rx[:, cols(half)], pl.rx[:, cols(half)]).then_inc(pl.ring_free, 1)

        with eng.Fori(0, DEPTH) as L:
            own = Own(eng, pl.dve_own, L * OWN_L, OWN_1)

            def scaled_out(dst, idx, half):
                eng.wait_ge(pl.ring_full, full(L, idx))
                dve.tensor_tensor(dst, pl.ring[:, bank(idx), 0:NH], pl.rx[:, cols(half)], ALU.mult) \
                    .then_inc(pl.ring_free, 1)

            def latent(b, half):
                dst = pl.cq[:, b, cols(half)] if b < 3 else pl.kv[:, b - 3, cols(half)]
                scaled_out(dst, (P1_A, P1_B)[half][b], half)

            eng.wait_ge(pl.ring_free, freed(L, -1))
            own.step(dve.tensor_tensor(pl.rx2[:, :], pl.rx[:, :], pl.rx[:, :], ALU.mult))
            for b in range(4):
                weight_lo(L, b, SLOT_P1[b])
            latent(0, 0)
            weight_lo(L, 4, SLOT_P1[4])
            for b in range(1, 4):
                latent(b, 0)
            latent(0, 1)
            latent(1, 1)
            weight_lo(L, 5, SLOT_P1[5])
            latent(2, 1)
            weight_lo(L, n_head(0, 0), SLOT_HD[0])
            latent(3, 1)
            weight_lo(L, n_head(0, 1), SLOT_HD[1])
            latent(4, 0)
            weight_lo(L, n_head(0, 2), SLOT_HD[2])
            small_lo(L, 0, SWE)
            inverted(pl.rk[:, 0, cols(0)], L, P1_SUM[0], 0)
            latent(4, 1)
            inverted(pl.rk[:, 0, cols(1)], L, P1_SUM[1], 1)
            eng.wait_ge(pl.ring_free, freed(L, P1_SUM[1]))
            for b in range(QC):
                dve.scalar_tensor_tensor(out=pl.cq[:, b, :], in0=pl.cq[:, b, :], scalar=pl.gain(L, G_Q + b),
                                         in1=pl.rk[:, 0, :], op0=ALU.mult, op1=ALU.mult).then_inc(pl.latent_f, 1)
            for b in range(QC):
                eng.wait_ge(pl.latent_hi, L * 5 + b + 1)
                minus(pl.cql[:, b, :], pl.cq[:, b, :], pl.cqh[:, b, :]).then_inc(pl.latent_lo, 1)
            eng.wait_ge(pl.tables_landed, L * 32 + 32)
            for half in range(2):
                cs, idx = cols(half), (P1_A, P1_B)[half][5]
                eng.wait_ge(pl.ring_full, full(L, idx))
                eng.wait_ge(pl.rope_swapped, L * 10 + half + 1)
                own.step(dve.tensor_tensor(pl.rope1_t[:, :], pl.ring[:, bank(idx), 0:NH], pl.cos[:, cs], ALU.mult))
                dve.tensor_tensor(pl.rope1_s[:, :], pl.rope1_s[:, :], pl.sin[:, cs], ALU.mult) \
                    .then_inc(pl.ring_free, 1)
                eng.wait_ge(pl.ring_free, freed(L, idx))
                own.step(dve.tensor_tensor(pl.rope1_t[:, :], pl.rope1_t[:, :], pl.rope1_s[:, :], ALU.add))
                own.wait()
                dve.tensor_tensor(pl.kpe[:, cs], pl.rope1_t[:, :], pl.rx[:, cs], ALU.mult).then_inc(pl.rope_sum, 1)
                inverted(pl.rk[:, 1, cs], L, P1_SUM[2 + half], 2 + half)
                eng.wait_ge(pl.rope_hi, L * 10 + half + 1)
                minus(pl.kel[:, cs], pl.kpe[:, cs], pl.keh[:, cs]).then_inc(pl.rope_lo, 1)
                if half == 0:
                    weight_lo(L, n_head(0, 3), SLOT_HD[3])
            eng.wait_ge(pl.ring_free, freed(L, P1_SUM[3]))
            for c in range(CC):
                dve.scalar_tensor_tensor(out=pl.kv[:, c, :], in0=pl.kv[:, c, :], scalar=pl.gain(L, G_KV + c),
                                         in1=pl.rk[:, 1, :], op0=ALU.mult, op1=ALU.mult).then_inc(pl.latent_f, 1)
            for c in range(CC):
                eng.wait_ge(pl.latent_hi, L * 5 + QC + c + 1)
                minus(pl.kvl[:, c, :], pl.kv[:, c, :], pl.kvh[:, c, :]).then_inc(pl.latent_lo, 1)
            own.done()

            with eng.Fori(0, HEADS // 2) as p:
                own = Own(eng, pl.dve_own, L * OWN_L + p * OWN_PAIR + OWN_1, OWN_PAIR)
                for e in range(2):
                    def of_head(per_head, j):
                        return L * (HEADS * per_head) + p * (2 * per_head) + (e * per_head + j + 1)

                    def ring_value(i, half, more):
                        return L * RING + p * 20 + (RING0 + r_hd(e, i, half) + 1 + more)

                    def entry(i, half):
                        eng.wait_ge(pl.ring_full, ring_value(i, half, RING))
                        return pl.ring[:, bank(r_hd(e, i, half)), 0:NH]

                    def head_out(dst, i, half, factor):
                        src = entry(i, half)
                        dve.tensor_tensor(dst, src, factor[:, cols(half)], ALU.mult).then_inc(pl.ring_free, 1)

                    def own_ring(i, half):
                        eng.wait_ge(pl.ring_free, ring_value(i, half, 4))

                    def next_weight(i):
                        n = n_head(e, 4) if i == 0 else n_head(e + 1, i - 1)
                        eng.wait_ge(pl.weights_hi, L * NB + p * 10 + (n + 1))
                        hi, lo, raw = pl.slot(SLOT_HD[4 if i == 0 else i - 1])
                        minus(lo, raw, hi).then_inc(pl.weights_lo, 1)

                    def proj_lo(j, lo, src, hi):
                        eng.wait_ge(pl.proj_hi, of_head(4, j))
                        minus(lo, src, hi).then_inc(pl.proj_lo, 1)

                    head_out(pl.gb[:, cols(0)], 0, 0, pl.rx)
                    head_out(pl.gb[:, cols(1)], 0, 1, pl.rx)
                    next_weight(0)
                    proj_lo(0, pl.kl[:, :], pl.att[:, 1024:1536], pl.kh[:, :])
                    proj_lo(1, pl.vl[:, :], pl.att[:, 1536:2048], pl.vh[:, :])
                    for half in range(2):
                        proj_lo(2 + half, pl.ql[:, cols(half)], pl.att[:, 512 * half:512 * half + NH],
                                pl.qh[:, cols(half)])
                    if e == 0:
                        for half in range(2):
                            cs, src = cols(half), pl.att[:, 512 * half:512 * half + NH]
                            eng.wait_ge(pl.projected, L * 40 + p * 10 + (4 + half + 1))
                            if half == 1:
                                eng.wait_ge(pl.rope_lo, L * 10 + p * 2 + 3)
                            eng.wait_ge(pl.rope_swapped, L * 10 + p * 2 + (2 + half + 1))
                            own.step(dve.tensor_tensor(pl.rope_t[:, :], src, pl.cos[:, cs], ALU.mult))
                            own.step(dve.tensor_tensor(pl.rope_s[:, :], pl.rope_s[:, :], pl.sin[:, cs], ALU.mult))
                            own.wait()
                            dve.tensor_tensor(pl.rope_t[:, :], pl.rope_t[:, :], pl.rope_s[:, :], ALU.add) \
                                .then_inc(pl.rope_sum, 1)
                            eng.wait_ge(pl.rope_hi, L * 10 + p * 2 + (2 + half + 1))
                            minus(pl.pel[:, cs], pl.rope_t[:, :], pl.peh[:, cs]).then_inc(pl.rope_lo, 1)
                    head_out(pl.ga[:, cols(0)], 1, 0, pl.rx)
                    head_out(pl.ga[:, cols(1)], 1, 1, pl.rx)
                    next_weight(1)
                    eng.wait_ge(pl.abs_hi, of_head(1, 0))
                    to = bass.ds(p * 128 + 64 * e, 64)
                    dve.tensor_tensor(pl.qal[:, :, to], pl.att[:, 1536:1664].rearrange("p (c q) -> p c q", c=2),
                                      pl.qah[:, :, to].bitcast(F32), ALU.subtract).then_inc(pl.abs_lo, 1)
                    for t in range(KT):
                        eng.wait_ge(pl.scored, of_head(4, max(t, 1)))
                        own.step(dve.memset(score_tile(pl, t)[0:CH, P * (t + 1) - CH:P * (t + 1)], NEG))
                    for t in range(KT):
                        own.wait(back=KT - 1)
                        own.step(dve.tensor_reduce(pl.mx[:, t:t + 1], score_tile(pl, t), AXX, ALU.max))
                    own.wait()
                    dve.tensor_scalar(pl.nmx[:, :], pl.mx[:, :], -SCALE, None, ALU.mult).then_inc(pl.row_max, 1)
                    head_out(pl.cv[:, cols(0)], 2, 0, pl.rx2)
                    eng.wait_ge(pl.exped, of_head(4, KT - 1))
                    own.step(dve.reciprocal(pl.ri[:, :], pl.rs[:, :]))
                    own.wait()
                    for t in range(KT):
                        tile = pl.probs[:, PO[t]:PO[t] + P * (t + 1)]
                        dve.tensor_scalar(tile, tile, pl.ri[:, t:t + 1], None, ALU.mult).then_inc(pl.normed, 1)
                    head_out(pl.cv[:, cols(1)], 2, 1, pl.rx2)
                    next_weight(2)
                    eng.wait_ge(pl.small_hi, L * 10 + p * 2 + (e + 2))
                    n = SWO if e == 0 else SWE
                    minus(pl.sl[:, 0:n], pl.sraw[:, 0:n], pl.sh[:, 0:n]).then_inc(pl.small_lo, 1)
                    for k, (src, at, n) in enumerate(TURNED):
                        eng.wait_ge(pl.turned_hi, of_head(3, k))
                        minus(pl.ptl[:, at:at + n], pl.att[:, src:src + n], pl.pth[:, at:at + n]) \
                            .then_inc(pl.turned_lo, 1)
                    dve.memset(pl.u[:, 0:2], 0.0)
                    dve.tensor_copy(pl.u[:, 2 + NP_:4 + NP_],
                                    pl.consts[:, bass.ds(L * (2 * KC) + p * 4 + (C_STATE + 2 * e), 2)])
                    own_ring(2, 1)
                    src = entry(3, 0)
                    dve.tensor_tensor(pl.u[:, 2:2 + NH], src, pl.cv[:, 0:NH], ALU.mult).then_inc(pl.ring_free, 1)
                    src = entry(3, 1)
                    dve.tensor_tensor(pl.u[:, 2 + NH:2 + NP_], src[:, 0:NP_ - NH], pl.cv[:, NH:NP_], ALU.mult)
                    dve.tensor_tensor(pl.u[:, 4 + NP_:4 + NT], src[:, NP_ - NH:NH], pl.cv[:, NP_:NT], ALU.mult) \
                        .then_inc(pl.ring_free, 1)
                    next_weight(3)
                    eng.wait_ge(pl.conv_first, of_head(1, 0))
                    for tap in (1, 2):
                        own.step(dve.scalar_tensor_tensor(out=pl.cv[:, :], in0=pl.u[:, tap:tap + NT + 2],
                                                          scalar=conv_weight(pl, L, p, e, tap), in1=pl.cv[:, :],
                                                          op0=ALU.mult, op1=ALU.add))
                        own.wait()
                    eng.wait_ge(pl.pv_made, of_head(1, 0))
                    dve.tensor_scalar(pl.sgb[:, p * 2 + e, :], pl.gb[:, NP_:NT], 1.0, None, ALU.add)
                    dve.scalar_tensor_tensor(out=pl.ybt[:, :], in0=pl.gb[:, 0:NP_], scalar=1.0,
                                             in1=pl.att[:, 1024:1536], op0=ALU.add, op1=ALU.mult) \
                        .then_inc(pl.pv_read, 1)
                    head_out(pl.bt[:, cols(0)], 4, 0, pl.rx)
                    head_out(pl.bt[:, cols(1)], 4, 1, pl.rx)
                    own_ring(4, 1)
                    dve.tensor_tensor(pl.bt[:, 0:NP_], pl.bt[:, 0:NP_], pl.cv[:, 0:NP_], ALU.mult)
                    own.step(dve.tensor_tensor(pl.bt[:, NP_:NT], pl.bt[:, NP_:NT], pl.cv[:, NP_ + 2:NT + 2],
                                               ALU.mult))
                    own.wait()
                    own.step(dve.scalar_tensor_tensor(out=pl.bt[:, :], in0=pl.ga[:, :], scalar=1.0, in1=pl.bt[:, :],
                                                      op0=ALU.add, op1=ALU.mult))
                    own.wait()
                    dve.tensor_copy(pl.my[:, p * 2 + e, NP_:NT], pl.bt[:, NP_:NT])
                    dve.tensor_tensor(pl.my[:, p * 2 + e, 0:NP_], pl.bt[:, 0:NP_], pl.ybt[:, :], ALU.add) \
                        .then_inc(pl.merged, 1)
                    next_weight(4)
                own.done()

            own = Own(eng, pl.dve_own, L * OWN_L + OWN_1 + OWN_PAIR * HEADS // 2, OWN_3)

            def merged_lo(i, m, t):
                eng.wait_ge(pl.x_hi, x_part(L, i))
                dve.scalar_tensor_tensor(out=pl.xl[:, m, t], in0=pl.my[:, m, t], scalar=0.5,
                                         in1=pl.xh[:, m, t].bitcast(F32), op0=ALU.mult, op1=ALU.subtract) \
                    .then_inc(pl.x_lo, 1)

            def cache_lo(i, lo, src, hi):
                eng.wait_ge(pl.cache_hi, L * 4 + i + 1)
                minus(lo, src, hi).then_inc(pl.cache_lo, 1)

            weight_lo(L, n_wo(4), SLOT_WO[4])
            for k in range(HEADS):
                merged_lo(X_WOA + k, k, cols(0))
            cache_lo(0, pl.ctl[:, :, :], pl.ctraw[:, :, :], pl.cth[:, :, :])
            cache_lo(1, pl.kcl[:, :], pl.kcraw[:, :], pl.kch[:, :])
            cache_lo(2, pl.nal[:, 0:4, :], pl.naraw[:, 0:4, :], pl.nah[:, 0:4, :])
            cache_lo(3, pl.nal[0:NS_, 4, :], pl.att[0:NS_, 1536:1792], pl.nah[0:NS_, 4, :])
            for k in range(HEADS):
                merged_lo(X_WOB + k, k, slice(NH, NP_))

            def s_max(t):
                eng.wait_ge(pl.s_scored, L * 4 + t + 1)
                own.step(dve.tensor_reduce(pl.stat[:, 0:1], pl.att[:, 0:NT], AXX, ALU.max))
                own.wait()
                dve.tensor_scalar(pl.stat[:, 1:2], pl.stat[:, 0:1], -SCALE, None, ALU.mult).then_inc(pl.s_max, 1)

            def s_normed(t):
                eng.wait_ge(pl.s_exped, L * 4 + t + 1)
                own.step(dve.reciprocal(pl.stat[:, 3:4], pl.stat[:, 2:3]))
                own.wait()
                dve.tensor_scalar(pl.ps[:, :], pl.ps[:, :], pl.stat[:, 3:4], None, ALU.mult).then_inc(pl.s_normed, 1)

            def s_turned_lo(t):
                eng.wait_ge(pl.s_thi, L * 4 + t + 1)
                minus(pl.tsl[:, 0:4, :], pl.att[:, 1024:1536].rearrange("p (k q) -> p k q", k=4), pl.tsh[:, 0:4, :])
                minus(pl.tsl[0:NS_, 4, :], pl.att[0:NS_, 576:704], pl.tsh[0:NS_, 4, :]).then_inc(pl.s_tlo, 1)

            def s_context_lo(t):
                eng.wait_ge(pl.s_chi, L * 4 + t + 1)
                minus(pl.ocl[:, :, :], pl.att[:, 1664:1920].rearrange("p (c q) -> p c q", c=2), pl.och[:, :, :]) \
                    .then_inc(pl.s_clo, 1)

            def s_merged(t):
                eng.wait_ge(pl.s_valued, L * 4 + t + 2)
                two = slice(2 * t, 2 * t + 2)
                own.step(dve.tensor_tensor(pl.ys[:, :, :], pl.att[:, 1920:2048].rearrange("p (h q) -> p h q", h=2),
                                           pl.sgb[:, two, :], ALU.mult))
                own.wait()
                dve.tensor_tensor(pl.my[:, two, NP_:NT], pl.my[:, two, NP_:NT], pl.ys[:, :, :], ALU.add) \
                    .then_inc(pl.s_merged, 1)
                merged_lo(X_WOS + t, two, slice(NP_, NT))

            def wo_out(idx, m, half):
                eng.wait_ge(pl.ring_full, full(L, idx))
                dve.tensor_copy(pl.my[:, m, cols(half)], pl.ring[:, bank(idx), 0:NH]).then_inc(pl.ring_free, 1)

            def residual(half, idx, post, pre, part, between=None):
                cs = cols(half)
                eng.wait_ge(pl.ring_free, freed(L, idx))
                for m in range(KC + 2):
                    if m < KC:
                        own.step(dve.tensor_tensor(pl.my[:, m, cs], pl.my[:, m, cs], pl.rx2[:, cs], ALU.mult))
                    if 1 <= m <= KC:
                        own.wait(back=1 if m < KC else 0)
                        dve.scalar_tensor_tensor(out=pl.x[:, m - 1, cs], in0=pl.my[:, m - 1, cs],
                                                 scalar=post(m - 1), in1=pl.x[:, m - 1, cs],
                                                 op0=ALU.mult, op1=ALU.add).then_inc(pl.x_new, 1)
                    if m >= 2:
                        eng.wait_ge(pl.x_hi, x_part(L, part + m - 2))
                        dve.scalar_tensor_tensor(out=pl.xl[:, m - 2, cs], in0=pl.x[:, m - 2, cs], scalar=pre(m - 2),
                                                 in1=pl.xh[:, m - 2, cs].bitcast(F32), op0=ALU.mult,
                                                 op1=ALU.subtract).then_inc(pl.x_lo, 1)
                    if between and m < KC:
                        between(m)

            s_max(0)
            s_normed(0)
            for m in range(4):
                wo_out(WO_A[m], m, 0)
            s_turned_lo(0)
            for t in (1, 2):
                for m in (0, 1):
                    wo_out(WO_A[2 * t + 2 + m], 2 * t + 2 + m, 0)
                    if (t, m) != (2, 1):
                        weight_lo(L, n_wo(3 + 2 * t + m), 3 + 2 * t + m)
                    if m == 0:
                        s_context_lo(t - 1)
                        s_max(t)
                        s_normed(t)
                s_merged(t - 1)
                s_turned_lo(t)
            s_context_lo(2)
            s_max(3)
            small_lo(L, 9, 1024)
            s_normed(3)
            inverted(pl.rx2[:, cols(0)], L, WO_SUM_A, 4)
            s_merged(2)
            s_turned_lo(3)
            s_context_lo(3)
            s_merged(3)
            ffn_gain = lambda m: pl.gain(L, G_FF + m)
            post_gain = lambda m: pl.gain(L, G_POST + m)

            residual(0, WO_SUM_A, post_gain, ffn_gain, X_FFA)
            for m in range(4):
                wo_out(WO_B[m], m, 1)
            for m, j in ((4, 0), (5, 1)):
                wo_out(WO_B[m], m, 1)
                weight_lo(L, n_w1(0, j), SLOT_W1[j])
            inverted(pl.rx[:, cols(0)], L, FF_SUM_A, 5)
            for m, j in ((6, 2), (7, 3)):
                wo_out(WO_B[m], m, 1)
                weight_lo(L, n_w1(0, j), SLOT_W1[j])
            own.done()

            own = Own(eng, pl.dve_own, L * OWN_L + OWN_1 + OWN_PAIR * HEADS // 2 + OWN_3, OWN_4)

            def hidden(ring_end, made, idx, parity, half, j):
                eng.wait_ge(pl.ring_full, ring_end + RING)
                dve.tensor_tensor(pl.ft[:, j % 2, :], pl.ring[:, bank(idx), 0:NH], pl.rx[:, cols(half)], ALU.mult) \
                    .then_inc(pl.ring_free, 1)
                eng.wait_ge(pl.ring_free, ring_end + 4)
                dve.scalar_tensor_tensor(out=pl.ff[:, j % 2, :], in0=pl.ft[:, j % 2, :], scalar=0.0,
                                         in1=pl.ft[:, j % 2, :], op0=ALU.max, op1=ALU.mult).then_inc(pl.f_made, 1)
                eng.wait_ge(pl.f_hi, made)
                minus(pl.fl[:, parity, j, cols(half)], pl.ff[:, j % 2, :], pl.fh[:, parity, j, cols(half)]) \
                    .then_inc(pl.f_lo, 1)

            def hidden_of(g, half, j):
                idx = r_w1(g, half, j)
                hidden(L * RING + (RING0 + idx + 1), L * 64 + (8 * g + 4 * half + j + 1), idx, g % 2, half, j)

            def w2_out(value, k, first=False):
                m, half = k % 8, k // 8
                eng.wait_ge(pl.w2_full, value)
                src, dst = pl.att[:, 512 * (k % 4):512 * (k % 4) + NH], pl.my[:, m, cols(half)]
                if first:
                    dve.tensor_copy(dst, src).then_inc(pl.w2_free, 1)
                else:
                    dve.tensor_tensor(dst, dst, src, ALU.add).then_inc(pl.w2_free, 1)

            eng.wait_ge(pl.ring_free, freed(L, FF_SUM_A))
            hidden_of(0, 0, 0)
            inverted(pl.rx2[:, cols(1)], L, WO_SUM_B, 6)
            residual(1, WO_SUM_B, post_gain, ffn_gain, X_FFB)
            for j in range(1, 4):
                hidden_of(0, 0, j)
            inverted(pl.rx[:, cols(1)], L, FF_SUM_B, 7)
            eng.wait_ge(pl.ring_free, freed(L, FF_SUM_B))
            for j in range(4):
                hidden_of(0, 1, j)
                if j >= 2:
                    weight_lo(L, n_w1(1, j - 2), SLOT_W1[j - 2])
            for k in range(8):
                hidden_of(1, k // 4, k % 4)
                if k < 2:
                    weight_lo(L, n_w1(1, k + 2), SLOT_W1[k + 2])
                elif k < 6:
                    weight_lo(L, n_w2(0, k - 2), SLOT_W2[k - 2])

            def group_weight(g, j, which):
                n = (n_w1(2, j), n_w2(1, j))[which]
                eng.wait_ge(pl.weights_hi, L * NB + g * 8 + (n + 1))
                hi, lo, raw = pl.slot((SLOT_W1, SLOT_W2)[which][j])
                minus(lo, raw, hi).then_inc(pl.weights_lo, 1)

            for k in range(16):
                w2_out(w2_filled(L, 0, k), k, first=True)
                if k % 4 == 2:
                    j = k // 4
                    weight_lo(L, n_w1(2, j), SLOT_W1[j])
            with eng.Fori(0, (GROUPS - 2) // 2) as i:
                for e in range(2):
                    for k in range(8):
                        idx = r_w1(2 + e, k // 4, k % 4)
                        hidden(L * RING + i * 16 + (RING0 + idx + 1), L * 64 + i * 16 + (8 * (e + 2) + k + 1),
                               idx, e, k // 4, k % 4)
                        if k % 2 == 1:
                            group_weight(i * 2 + e, k // 2, 1)
                    for k in range(16):
                        w2_out(L * W2N + i * 32 + (W2N + 16 * (e + 1) + k + 1), k)
                        if k % 4 == 2:
                            group_weight(i * 2 + (e + 1), k // 4, 0)
            g = GROUPS - 1
            next_gain = lambda m: pl.gain(L, G_PRE + m, 1)
            ffn_post_gain = lambda m: pl.gain(L, G_FPOST + m)
            for k in range(8):
                w2_out(w2_filled(L, g, k), k)
            inverted(pl.rx2[:, cols(0)], L, END_SUM[0], 8)
            residual(0, END_SUM[0], ffn_post_gain, next_gain, X_NXA,
                     between=lambda m: w2_out(w2_filled(L, g, 8 + m), 8 + m))
            inverted(pl.rx[:, cols(0)], L, END_SUM[1], 9)
            inverted(pl.rx2[:, cols(1)], L, END_SUM[2], 10)
            residual(1, END_SUM[2], ffn_post_gain, next_gain, X_NXB)
            inverted(pl.rx[:, cols(1)], L, END_SUM[3], 11)
            own.done()


def tensor_engine(nc, block, pl):
    pe = nc.tensor
    ones, ident = pl.const(C_ONE, P), pl.const(C_ID, P)
    att = pl.att

    def rows_of(pair, *at):
        return pair[0][at], pair[1][at]

    xs, small = (pl.xh, pl.xl), (pl.sh, pl.sl)
    cqn, ckv, kpe = (pl.cqh, pl.cql), (pl.kvh, pl.kvl), (pl.keh, pl.kel)
    q, q_pe, k_, v = (pl.qh, pl.ql), (pl.peh, pl.pel), (pl.kh, pl.kl), (pl.vh, pl.vl)
    probs_t = (pl.pth, pl.ptl)
    q_abs, q_pe_sample = (pl.qah, pl.qal), (pl.qph, pl.qpl)
    cache_t, cache_pe, cache_n = (pl.cth, pl.ctl), (pl.kch, pl.kcl), (pl.nah, pl.nal)
    probs_s_t, context, f = (pl.tsh, pl.tsl), (pl.och, pl.ocl), (pl.fh, pl.fl)
    ALL = slice(0, P)

    @block.tensor
    def _(eng):
        eng.wait_ge(pl.consts_landed, 16)
        for half in range(2):
            eng.wait_ge(pl.ring_free, half + 1)
            eng.wait_ge(pl.summed, 2 * KC + half + 1)
            pe.matmul(pl.ring[:, half, 0:NH], ones, pl.ss[:, half, :], start=True, stop=True) \
                .then_inc(pl.ring_full, 1)

        with eng.Fori(0, DEPTH) as L:
            def block_half(L_ring, idx, s, half, weight=None, x_ready=None, k0=0, k1=KC):
                if k0 == 0:
                    eng.wait_ge(pl.ring_free, L_ring + (RING0 + idx + 1))
                if weight is not None:
                    eng.wait_ge(pl.weights_lo, weight)
                hi, lo, _ = pl.slot(s)
                out = pl.ring[:, bank(idx), 0:NH]
                for k in range(k0, k1):
                    if x_ready:
                        eng.wait_ge(pl.x_lo, x_ready(k))
                    w = slice(k * P, (k + 1) * P)
                    last = mm3(pe, out, (hi[:, w], lo[:, w]), rows_of(xs, ALL, k, cols(half)), k == 0, k == KC - 1)
                if k1 == KC:
                    last.then_inc(pl.ring_full, 1)

            def norm_sum(idx, ss, k):
                eng.wait_ge(pl.ring_free, may_fill(L, idx))
                eng.wait_ge(pl.summed, square(L, k) + 2)
                pe.matmul(pl.ring[:, bank(idx), 0:NH], ones, ss, start=True, stop=True).then_inc(pl.ring_full, 1)

            def latent_block(b, half):
                block_half(L * RING, (P1_A, P1_B)[half][b], SLOT_P1[b], half, L * NB + (b + 1))

            eng.wait_ge(pl.x_lo, L * 52 + 8)
            for half in range(2):
                for b in range(4):
                    latent_block(b, half)
            latent_block(4, 0)
            norm_sum(P1_SUM[0], pl.ss1[:, 0, :], S_CQA + 2)
            latent_block(4, 1)
            norm_sum(P1_SUM[1], pl.ss1[:, 1, :], S_CQB + 2)
            latent_block(5, 0)
            norm_sum(P1_SUM[2], pl.ss1[:, 2, :], S_KVA1)
            latent_block(5, 1)
            norm_sum(P1_SUM[3], pl.ss1[:, 3, :], S_KVB1)

            with eng.Fori(0, HEADS // 2) as p:
                for e in range(2):
                    def of_head(per_head, j):
                        return L * (HEADS * per_head) + p * (2 * per_head) + (e * per_head + j + 1)

                    def head_block(i):
                        for half in range(2):
                            block_half(L * RING + p * 20, r_hd(e, i, half), SLOT_HD[i], half,
                                       L * NB + p * 10 + (n_head(e, i) + 1) if half == 0 else None)

                    def small_w(at, c):
                        return rows_of(small, ALL, slice(at + c * P, at + (c + 1) * P))

                    def query(at, half):
                        out = att[:, 512 * half:512 * half + NH]
                        for k in range(QC):
                            last = mm3(pe, out, small_w(at, k), rows_of(cqn, ALL, k, cols(half)), k == 0, k == QC - 1)
                        last.then_inc(pl.projected, 1)

                    head_block(0)
                    eng.wait_ge(pl.small_lo, L * 10 + p * 2 + (e + 1))
                    eng.wait_ge(pl.latent_lo, L * 5 + 5)
                    eng.wait_ge(pl.pv_read, L * HEADS + p * 2 + (e + 1))
                    for c in range(CC):
                        last = mm3(pe, att[:, 1024:1536], small_w(UK, c), rows_of(ckv, ALL, c, slice(0, NP_)),
                                   c == 0, c == CC - 1)
                    last.then_inc(pl.projected, 1)
                    for kt in range(KT):
                        keys = slice(P * kt, P * (kt + 1))
                        for c in range(CC):
                            last = mm3(pe, att[:, 1536 + P * kt:1536 + P * (kt + 1)], rows_of(ckv, ALL, c, keys),
                                       small_w(UV, c), c == 0, c == CC - 1)
                    last.then_inc(pl.projected, 1)
                    query(UQ, 0)
                    query(UQ, 1)
                    if e == 0:
                        eng.wait_ge(pl.proj_lo, of_head(4, 3))
                        query(UPE, 0)
                        query(UPE, 1)
                    head_block(1)
                    eng.wait_ge(pl.proj_lo, of_head(4, 3))
                    if e == 0:
                        eng.wait_ge(pl.rope_lo, L * 10 + p * 2 + 4)
                    for c in range(CC):
                        last = mm3(pe, att[:, 1536 + 64 * c:1536 + 64 * (c + 1)], small_w(UKT, c),
                                   rows_of(q, ALL, slice(NP_, NT)), True, True)
                    last.then_inc(pl.absorbed, 1)
                    half_rows = slice(64 * e, 64 * e + 64)
                    for t in range(KT):
                        tile, keys = slice(P * t, P * (t + 1)), slice(0, P * (t + 1))
                        mm3(pe, score_tile(pl, t), rows_of(q, ALL, tile), rows_of(k_, ALL, keys), True, False)
                        mm3(pe, score_tile(pl, t), rows_of(q_pe, half_rows, tile), rows_of(kpe, half_rows, keys),
                            False, True).then_inc(pl.scored, 1)
                    head_block(2)
                    eng.wait_ge(pl.normed, of_head(4, KT - 1))
                    eng.wait_ge(pl.abs_lo, of_head(1, 0))
                    for j, at in enumerate((1536, 0, 512, 768)):
                        for t in range(j, KT):
                            to = at + P * (t - j)
                            last = pe.transpose(att[:, to:to + P], pl.probs[:, PO[t] + P * j:PO[t] + P * (j + 1)], ident)
                        if j != 2:
                            last.then_inc(pl.turned, 1)
                    head_block(3)
                    eng.wait_ge(pl.turned_lo, of_head(3, 2))
                    for j in range(KT):
                        n = NP_ - P * j
                        last = mm3(pe, att[:, 1024 + P * j:1536], rows_of(v, ALL, slice(P * j, P * (j + 1))),
                                   rows_of(probs_t, ALL, slice(PTO[j], PTO[j] + n)), j == 0, j == KT - 1)
                    last.then_inc(pl.pv_made, 1)
                    head_block(4)

            def wo(m, half, k0=0, k1=KC, ready=None):
                weight = L * NB + (n_wo(m) + 1) if half == 0 and k0 == 0 else None
                block_half(L * RING, (WO_A, WO_B)[half][m], SLOT_WO[m], half, weight, ready, k0, k1)

            def merged_a(k):
                return x_part(L, X_WOA + k)

            def merged_b(k):
                return x_part(L, X_WOS + k // 2)

            def s_scores(t):
                if t == 0:
                    eng.wait_ge(pl.pe_sample, L * 16 + 16)
                    eng.wait_ge(pl.cache_lo, L * 4 + 2)
                    eng.wait_ge(pl.abs_lo, L * HEADS + HEADS)
                else:
                    eng.wait_ge(pl.s_exped, L * 4 + t)
                two = slice(P * t, P * (t + 1))
                for out, latents, rotary, keys in ((att[:, 0:PAST], cache_t, cache_pe, slice(0, PAST)),
                                                   (att[:, PAST:PAST + NS_], ckv, kpe, slice(NP_, NT))):
                    for c in range(CC):
                        mm3(pe, out, rows_of(q_abs, ALL, c, two), rows_of(latents, ALL, c, keys), c == 0, False)
                    last = mm3(pe, out, rows_of(q_pe_sample, slice(0, ROPE), two),
                               rows_of(rotary, slice(0, ROPE), keys), False, True)
                last.then_inc(pl.s_scored, 1)

            def s_turn(t):
                eng.wait_ge(pl.s_normed, L * 4 + t + 1)
                if t == 0:
                    eng.wait_ge(pl.pv_read, L * HEADS + HEADS + 1)
                for j in range(4):
                    pe.transpose(att[:, 1024 + P * j:1024 + P * (j + 1)], pl.ps[:, P * j:P * (j + 1)], ident)
                pe.transpose(att[0:NS_, 576:704], pl.ps[:, PAST:NT], ident).then_inc(pl.s_turned, 1)

            def s_attend(t):
                eng.wait_ge(pl.s_tlo, L * 4 + t + 1)
                if t == 0:
                    eng.wait_ge(pl.cache_lo, L * 4 + 4)
                else:
                    eng.wait_ge(pl.s_merged, L * 4 + t)
                for c in range(CC):
                    for kt in range(5):
                        rows = slice(0, P if kt < 4 else NS_)
                        last = mm3(pe, att[:, 1664 + P * c:1664 + P * (c + 1)],
                                   rows_of(cache_n, rows, kt, slice(P * c, P * (c + 1))),
                                   rows_of(probs_s_t, rows, kt, ALL), kt == 0, kt == 4)
                last.then_inc(pl.s_context, 1)

            def s_values(t):
                eng.wait_ge(pl.s_clo, L * 4 + t + 1)
                eng.wait_ge(pl.small_lo, L * 10 + (9 if t < 2 else 10))
                for hh in range(2):
                    for c in range(CC):
                        at = ((2 * t + hh) % 4 * 2 + c) * P
                        last = mm3(pe, att[:, 1920 + 64 * hh:1920 + 64 * (hh + 1)],
                                   rows_of(small, ALL, slice(at, at + P)),
                                   rows_of(context, ALL, c, slice(64 * hh, 64 * (hh + 1))), c == 0, c == CC - 1)
                last.then_inc(pl.s_valued, 1)

            eng.wait_ge(pl.sample_kept, L + 1)
            eng.sem_inc(pl.waits_apart, 1)
            for c in range(CC):
                last = pe.transpose(att[0:NS_, 1536 + P * c:1536 + P * (c + 1)], pl.kv_sample[:, c, :], ident)
            last.then_inc(pl.new_turned, 1)
            for m in range(4):
                wo(m, 0, 0, 4, merged_a)
            s_scores(0)
            for m in range(4):
                wo(m, 0, 4, KC, merged_a)
            s_turn(0)
            for t in range(2):
                wo(4 + 2 * t, 0)
                s_attend(t)
                s_scores(t + 1)
                wo(5 + 2 * t, 0)
                s_values(t)
                s_turn(t + 1)
            for m in range(2):
                wo(m, 1, 0, 4, merged_b)
            s_attend(2)
            s_scores(3)
            wo(2, 1, 0, 4)
            norm_sum(WO_SUM_A, pl.ss[:, 0, :], S_POSTA + 7)
            s_values(2)
            s_turn(3)
            wo(3, 1, 0, 4)
            for m in range(3):
                wo(m, 1, 4, 6, merged_b)
            s_attend(3)
            wo(3, 1, 4, 6)
            s_values(3)
            for m in range(4):
                wo(m, 1, 6, KC, merged_b)
            wo(4, 1)
            wo(5, 1)
            norm_sum(FF_SUM_A, pl.ss[:, 0, :], S_PREA + 7)
            wo(6, 1)
            wo(7, 1)

            def w1_first(half, j):
                weight = L * NB + (n_w1(0, j) + 1) if half == 0 else None
                block_half(L * RING, r_w1(0, half, j), SLOT_W1[j], half, weight)

            def w1(L_ring, L_weight, g):
                for half in range(2):
                    for j in range(4):
                        weight = L_weight + (n_w1(g, j) + 1) if half == 0 else None
                        block_half(L_ring, r_w1(g, half, j), SLOT_W1[j], half, weight)

            def w2_block(free, f_ready, weight, slots, parity, m, half):
                k_ring = 8 * half + m
                eng.wait_ge(pl.w2_free, free + k_ring)
                if m == 0:
                    eng.wait_ge(pl.f_lo, f_ready + 4 * (half + 1))
                if half == 0 and m % 2 == 0:
                    eng.wait_ge(pl.weights_lo, weight + m // 2)
                hi, lo, _ = pl.slot(slots[m // 2])
                out = att[:, 512 * (k_ring % 4):512 * (k_ring % 4) + NH]
                for k in range(4):
                    at = k * 256 + m % 2 * P
                    last = mm3(pe, out, (hi[:, at:at + P], lo[:, at:at + P]), rows_of(f, ALL, parity, k, cols(half)),
                               k == 0, k == 3)
                last.then_inc(pl.w2_full, 1)

            eng.wait_ge(pl.x_lo, x_part(L, X_FFA + 7))
            w1_first(0, 0)
            norm_sum(WO_SUM_B, pl.ss[:, 1, :], S_POSTB + 7)
            for j in range(1, 4):
                w1_first(0, j)
            norm_sum(FF_SUM_B, pl.ss[:, 1, :], S_PREB + 7)
            eng.wait_ge(pl.x_lo, x_part(L, X_FFB + 7))
            for j in range(4):
                w1_first(1, j)
            w1(L * RING, L * NB, 1)

            def w2(L_w2, L_f, L_weight, g):
                for half in range(2):
                    for m in range(KC):
                        w2_block(L_w2 + (16 * g + 1), L_f + 8 * g, L_weight + (n_w2(g, 0) + 1), SLOT_W2, g % 2,
                                 m, half)

            w2(L * W2N, L * 64, L * NB, 0)
            with eng.Fori(0, (GROUPS - 2) // 2) as i:
                for e in range(2):
                    w1(L * RING + i * 16, L * NB + i * 16, 2 + e)
                    w2(L * W2N + i * 32, L * 64 + i * 16, L * NB + i * 16, 1 + e)
            g = GROUPS - 1

            def last_w2(m, half):
                w2_block(L * W2N + (16 * g + 1), L * 64 + 8 * g, L * NB + (n_w2(g, 0) + 1), SLOT_W1, g % 2, m, half)

            for m in range(KC):
                last_w2(m, 0)
            last_w2(0, 1)
            norm_sum(END_SUM[0], pl.ss[:, 0, :], S_FPA + 7)
            for m in range(1, KC):
                last_w2(m, 1)
            norm_sum(END_SUM[1], pl.ss[:, 0, :], S_MIX + 14)
            norm_sum(END_SUM[2], pl.ss[:, 1, :], S_MIX + 15)
            norm_sum(END_SUM[3], pl.ss[:, 1, :], S_NXB + 7)


def kernel(x_prompt, x_sample, cache_ckv, cache_kpe, state_conv, w_in, conv_w, w_uq, w_uk, w_uv, w_o, w1, w2,
           g_pre_mix, g_post_mix, g_pre_ffn, g_post_ffn, g_q, g_kv):
    import concourse.bacc as bacc
    from concourse.bass_utils import run_bass_kernel_spmd

    def array(a):
        return np.asarray(a, dtype=np.float32)

    def per_feature(a):
        return a.reshape(a.shape[0] // P, P, *a.shape[1:]).swapaxes(0, 1)

    x = np.concatenate([array(x_prompt)[0], array(x_sample)[0]])
    x_in = per_feature(x.T)

    consts = np.zeros((P, N_CONST), np.float32)
    consts[:, C_ID:C_ID + P] = np.eye(P, dtype=np.float32)
    consts[:, C_ONE:C_ONE + P] = 1.0
    consts[:, C_EPS] = EPS
    for L in range(DEPTH):
        at = C_GAIN + L * NG
        for col, g in ((G_PRE, g_pre_mix), (G_POST, g_post_mix), (G_FF, g_pre_ffn), (G_FPOST, g_post_ffn),
                       (G_Q, g_q), (G_KV, g_kv)):
            a = per_feature(array(g)[L])
            consts[:, at + col:at + col + a.shape[1]] = a
        taps = per_feature(array(conv_w)[L].T)
        consts[:, at + G_CONV:at + G_CONV + 3 * KC] = taps.reshape(P, 3 * KC)
        state = per_feature(array(state_conv)[L, 0].T)
        consts[:, C_STATE + L * 2 * KC:C_STATE + (L + 1) * 2 * KC] = state.reshape(P, 2 * KC)

    inv = (10000.0 ** (-np.arange(0, ROPE, 2) / ROPE)).astype(np.float32)
    angles = np.arange(NT, dtype=np.float32)[None, :] * inv[np.arange(P) % 32][:, None]
    sign = np.where(np.arange(P) // 32 % 2 == 0, -1.0, 1.0).astype(np.float32)[:, None]
    tables = np.stack([np.cos(angles), np.sin(angles) * sign]).astype(np.float32)

    blocks = np.zeros((DEPTH * NB, P, 1024), np.float32)

    def block(n, w):
        blocks[n] = per_feature(w).reshape(P, 1024)

    off_c, off_x, off_q = D, 2 * D, 3 * D
    off_kv = off_q + QL
    off_pe = off_kv + KL
    off_ga = off_pe + ROPE
    off_gb = off_ga + D
    for L in range(DEPTH):
        w, wo, up, down = array(w_in)[L], array(w_o)[L], array(w1)[L], array(w2)[L]
        base = L * NB
        for b in range(QC + CC):
            block(base + b, w[:, off_q + b * P:off_q + (b + 1) * P])
        rotary = w[:, off_pe:off_pe + ROPE]
        block(base + 5, np.concatenate([rotary, rotary], 1))
        for h in range(HEADS):
            for i, off in enumerate((off_gb, off_ga, off_c, off_x, 0)):
                block(base + n_head(h, i), w[:, off + h * P:off + (h + 1) * P])
        for m in range(KC):
            block(base + n_wo(m), wo[:, m * P:(m + 1) * P])
        for g in range(GROUPS):
            for j in range(4):
                block(base + n_w1(g, j), up[:, (4 * g + j) * P:(4 * g + j + 1) * P])
                block(base + n_w2(g, j), down[4 * g * P:4 * (g + 1) * P, j * 256:(j + 1) * 256])

    small = np.zeros((DEPTH * 5, P, SWE + SWO), np.float32)
    uv = np.zeros((DEPTH, P, 1024), np.float32)
    for L in range(DEPTH):
        uq = array(w_uq)[L].reshape(QL, HEADS, QK)
        uk = array(w_uk)[L].reshape(KL, HEADS, NOPE)
        uvs = array(w_uv)[L].reshape(KL, HEADS, P)
        for h in range(HEADS):
            to = small[L * 5 + h // 2][:, SWE * (h % 2):]
            to[:, UQ:UQ + QC * P] = per_feature(uq[:, h, 0:NOPE]).reshape(P, QC * P)
            to[:, UK:UK + CC * P] = per_feature(uk[:, h]).reshape(P, CC * P)
            to[:, UV:UV + CC * P] = per_feature(uvs[:, h]).reshape(P, CC * P)
            to[:, UKT:UKT + KL] = uk[:, h].T
            if h % 2 == 0:
                both = np.concatenate([uq[:, h, NOPE:], uq[:, h + 1, NOPE:]], 1)
                to[:, UPE:UPE + QC * P] = per_feature(both).reshape(P, QC * P)
        values = per_feature(uvs).transpose(0, 2, 1, 3)
        small[L * 5 + 4, :, 0:1024] = values[:, 0:4].reshape(P, 1024)
        uv[L] = values[:, 4:8].reshape(P, 1024)

    ckv, kpe = array(cache_ckv)[:, 0], array(cache_kpe)[:, 0]
    cache_t = ckv.transpose(0, 2, 1).reshape(DEPTH, CC, P, PAST).transpose(0, 2, 1, 3)
    cache_n = ckv.reshape(DEPTH, PAST // P, P, KL).transpose(0, 2, 1, 3)
    cache_pe = kpe.transpose(0, 2, 1)

    nc = bacc.Bacc("TRN2", target_bir_lowering=False, num_devices=1, dynamic_dma_scratch_size=1024)
    arrays, args = {}, []
    for name, a in (("x", x_in), ("consts", consts), ("tables", tables), ("blocks", blocks), ("small", small),
                    ("uv", uv), ("cache_t", cache_t), ("cache_n", cache_n), ("cache_pe", cache_pe)):
        arrays[name + "_in"] = np.ascontiguousarray(a)
        args.append(nc.dram_tensor(name + "_in", a.shape, F32, kind="ExternalInput").ap())
    for name, shape in (("x", (P, KC, NT)), ("kv", (DEPTH, P, CC, NT)), ("kpe", (DEPTH, ROPE, NT)),
                        ("conv", (DEPTH, P, KC, 4))):
        args.append(nc.dram_tensor(name + "_out", shape, F32, kind="ExternalOutput").ap())
    program(nc, *args)
    r = run_bass_kernel_spmd(nc, [arrays], core_ids=[0]).results[0]

    y = r["x_out"].transpose(2, 1, 0).reshape(NT, D)
    kv = r["kv_out"].transpose(0, 3, 2, 1).reshape(DEPTH, 1, NT, KL)
    pe_new = r["kpe_out"].transpose(0, 2, 1)[:, None]
    conv = r["conv_out"].transpose(0, 3, 2, 1).reshape(DEPTH, 1, 4, D)
    return (y[None, 0:NP_], y[None, NP_:], kv[:, :, 0:NP_], pe_new[:, :, 0:NP_], conv[:, :, 0:2],
            kv[:, :, NP_:], pe_new[:, :, NP_:], conv[:, :, 2:4])
```

```python
from contextlib import ExitStack

import numpy as np

import concourse.bass as bass
from concourse import mybir

F32 = mybir.dt.float32
F32R = mybir.dt.float32r
ALU = mybir.AluOpType
ACT = mybir.ActivationFunctionType
AXX = mybir.AxisListType.X

P = 128
D = 1024
DEPTH = 2
NP_, NS_ = 512, 64
NT = NP_ + NS_
NH = 288
PAST = 512
HEADS = 8
QL, KL = 384, 256
NOPE, ROPE = 128, 64
QK = NOPE + ROPE
DFF = 4 * D
CH = 64
EPS = 1e-6
SCALE = float(QK) ** -0.5
NEG = -1e30
KC = D // P
QC, CC = QL // P, KL // P
KT = NP_ // P
GROUPS = DFF // 512

N_P1, N_HEAD, N_WO, N_GRP = 6, 5, 8, 4
NB = N_P1 + N_HEAD * HEADS + N_WO + 2 * N_GRP * GROUPS
SLOT_P1 = [4, 1, 2, 3, 0, 4]
SLOT_HD = [1, 2, 3, 0, 4]
SLOT_WO = [1, 2, 3, 0, 4, 5, 6, 7]
SLOT_W1 = [1, 2, 3, 0]
SLOT_W2 = [4, 5, 6, 7]
SLOT_USES = [19, 19, 19, 19, 18, 8, 8, 8]


EARLY = (1, 2, 3)


def n_head(h, i):
    return N_P1 + N_HEAD * h + i


def n_wo(m):
    return N_P1 + N_HEAD * HEADS + m


def n_w1(g, j):
    return n_wo(8) + j if g == 0 else n_wo(8) + 8 * g - 4 + j


def n_w2(g, j):
    return n_wo(8) + 8 + 8 * g + j if g < GROUPS - 1 else NB - 4 + j


def use_p1(b):
    return 2 if b == 5 else 1


def use_hd(h, i):
    return h + (3 if SLOT_HD[i] == 4 else 2)


def use_wo(m):
    s = SLOT_WO[m]
    return 11 if s == 4 else 10 if s < 4 else 1


def use_w1(g, j):
    return g + 11


def use_w2(g, j):
    return g + (12 if SLOT_W2[j] == 4 else 2)


RING = 184
POST_SUM_B = 0
P1_A, P1_B = [1, 3, 4, 5, 11, 15], [6, 8, 9, 10, 13, 17]
PRE_SUM = [2, 7]
P1_SUM = [12, 14, 16, 18]
HD0 = 19


def r_hd(h, i, s):
    return HD0 + 10 * h + 2 * i + s


R3 = HD0 + 10 * HEADS
WO_A = [R3 + m for m in range(8)]
WO_SUM_A = R3 + 8
WO_B = [R3 + m for m in range(9, 17)]
FF_SUM_A = R3 + 17
FF_A = [R3 + m for m in (18, 20, 21, 22)]
WO_SUM_B = R3 + 19
FF_SUM_B = R3 + 24
FF_B = [R3 + m for m in (23, 25, 26, 27)]


def r_w1(g, s, j):
    return (FF_A, FF_B)[s][j] if g == 0 else R3 + 28 + 8 * (g - 1) + 4 * s + j


W2N = 16 * GROUPS
POST_SUM_A, NEXT_SUM_B = RING - 1, RING
assert r_w1(GROUPS - 1, 1, 3) == RING - 2

G_PRE, G_POST, G_FF, G_FPOST, G_Q, G_KV, G_CONV = 0, 8, 16, 24, 32, 35, 37
NG = 37 + 24
SWE, SWO = 1536, 1152
UQ, UK, UV, UKT, UPE = 0, 384, 640, 896, 1152
PO = [0, 128, 384, 768]
PTO = [0, 512, 896, 1152]


PCOLS = sum(P * (t + 1) for t in range(KT))
C_ID, C_ONE, C_EPS, C_GAIN = 0, P, 2 * P, 2 * P + 1 + NG
C_STATE = C_GAIN + (DEPTH + 1) * NG
N_CONST = C_STATE + DEPTH * KC * 2
OWN_1, OWN_PAIR, OWN_3, OWN_4 = 14, 30, 20, 17
OWN_L = OWN_1 + (HEADS // 2) * OWN_PAIR + OWN_3 + OWN_4


def bank(idx):
    return idx % 4


class Plan:

    def __init__(self, nc, ctx):
        self.nc = nc
        self.memory()
        self.ring = ctx.enter_context(nc.psum_tensor("ring", [P, 4, 512], F32))
        self.att = ctx.enter_context(nc.psum_tensor("att", [P, 4 * 512], F32))

        def semaphore(name):
            return ctx.enter_context(nc.semaphore(name))

        self.consts_landed = semaphore("consts_landed")
        self.x_landed0 = semaphore("x_landed0")
        self.x_landed1 = semaphore("x_landed1")
        self.x_landed2 = semaphore("x_landed2")
        self.x_landed3 = semaphore("x_landed3")
        self.x_landed4 = semaphore("x_landed4")
        self.x_landed5 = semaphore("x_landed5")
        self.x_landed6 = semaphore("x_landed6")
        self.x_landed7 = semaphore("x_landed7")
        self.tables_landed = semaphore("tables_landed")
        self.small_landed = semaphore("small_landed")
        self.cache_landed = semaphore("cache_landed")
        self.nat_landed = semaphore("nat_landed")
        self.slot0 = semaphore("slot0")
        self.slot1 = semaphore("slot1")
        self.slot2 = semaphore("slot2")
        self.slot3 = semaphore("slot3")
        self.slot4 = semaphore("slot4")
        self.slot5 = semaphore("slot5")
        self.slot6 = semaphore("slot6")
        self.slot7 = semaphore("slot7")
        self.weights_hi = semaphore("weights_hi")
        self.weights_lo = semaphore("weights_lo")
        self.early_lo = semaphore("early_lo")
        self.small_hi = semaphore("small_hi")
        self.small_lo = semaphore("small_lo")
        self.ring_full = semaphore("ring_full")
        self.ring_free = semaphore("ring_free")
        self.w2_full = semaphore("w2_full")
        self.w2_free = semaphore("w2_free")
        self.squared = semaphore("squared")
        self.summed = semaphore("summed")
        self.rooted = semaphore("rooted")
        self.x_hi = semaphore("x_hi")
        self.x_lo = semaphore("x_lo")
        self.x_new = semaphore("x_new")
        self.latent_f = semaphore("latent_f")
        self.latent_hi = semaphore("latent_hi")
        self.latent_lo = semaphore("latent_lo")
        self.rope_swapped = semaphore("rope_swapped")
        self.rope_sum = semaphore("rope_sum")
        self.rope_hi = semaphore("rope_hi")
        self.rope_lo = semaphore("rope_lo")
        self.sample_kept = semaphore("sample_kept")
        self.projected = semaphore("projected")
        self.proj_hi = semaphore("proj_hi")
        self.proj_lo = semaphore("proj_lo")
        self.absorbed = semaphore("absorbed")
        self.abs_hi = semaphore("abs_hi")
        self.abs_lo = semaphore("abs_lo")
        self.pe_sample = semaphore("pe_sample")
        self.scored = semaphore("scored")
        self.row_max = semaphore("row_max")
        self.exped = semaphore("exped")
        self.normed = semaphore("normed")
        self.turned = semaphore("turned")
        self.turned_hi = semaphore("turned_hi")
        self.turned_lo = semaphore("turned_lo")
        self.pv_made = semaphore("pv_made")
        self.pv_read = semaphore("pv_read")
        self.gated = semaphore("gated")
        self.conv_first = semaphore("conv_first")
        self.merged = semaphore("merged")
        self.cache_hi = semaphore("cache_hi")
        self.cache_lo = semaphore("cache_lo")
        self.new_turned = semaphore("new_turned")
        self.s_scored = semaphore("s_scored")
        self.s_max = semaphore("s_max")
        self.s_exped = semaphore("s_exped")
        self.s_normed = semaphore("s_normed")
        self.s_turned = semaphore("s_turned")
        self.s_thi = semaphore("s_thi")
        self.s_tlo = semaphore("s_tlo")
        self.s_context = semaphore("s_context")
        self.s_chi = semaphore("s_chi")
        self.s_clo = semaphore("s_clo")
        self.s_valued = semaphore("s_valued")
        self.s_merged = semaphore("s_merged")
        self.f_made = semaphore("f_made")
        self.f_hi = semaphore("f_hi")
        self.f_lo = semaphore("f_lo")
        self.latents_stored = semaphore("latents_stored")
        self.conv_stored = semaphore("conv_stored")
        self.x_stored = semaphore("x_stored")
        self.dve_own = semaphore("dve_own")
        self.waits_apart = semaphore("waits_apart")
        self.slots = [self.slot0, self.slot1, self.slot2, self.slot3, self.slot4, self.slot5, self.slot6, self.slot7]
        self.x_landed = [self.x_landed0, self.x_landed1, self.x_landed2, self.x_landed3,
                         self.x_landed4, self.x_landed5, self.x_landed6, self.x_landed7]

    def memory(self):
        start = (self.nc.sbuf_base + 31) // 32 * 32
        top = self.nc.sbuf_usable_end
        mark = [start]

        def put(name, shape, dt=F32):
            size = (4 * int(np.prod(shape[1:])) + 31) // 32 * 32
            at = mark[0]
            mark[0] = at + size
            assert mark[0] <= top, f"{name} ends {mark[0] - top} bytes past the end"
            return self.nc.alloc_sbuf_tensor_at(name, shape, dt, offset=at)

        def split(name, shape, raw=False):
            hi = put(name + "_hi", shape, F32R)
            at = mark[0]
            lo = put(name + "_lo", shape, F32R)
            if not raw:
                return hi, lo
            return hi, lo, self.nc.alloc_sbuf_tensor_at(name + "_raw", shape, F32, offset=at)

        self.x = put("x", [P, KC, NT])
        self.consts = put("consts", [P, N_CONST])
        self.rx, self.rx2 = put("rx", [P, NT]), put("rx2", [P, NT])
        self.conv_tail = put("conv_tail", [P, KC, 4])
        self.kv_sample = put("kv_sample", [P, CC, NS_])
        self.xh, self.xl = split("xs", [P, KC, NT])
        self.my = put("my", [P, KC, NT])
        self.sh, self.sl, self.sraw = split("small", [P, SWE], raw=True)
        self.wh, self.wl, self.wraw = split("w", [P, 5, 1024], raw=True)
        self.qah, self.qal = split("q_abs", [P, CC, HEADS * NS_])
        self.qph, self.qpl = split("q_pe_sample", [ROPE, HEADS * NS_])
        self.sgb = put("gate_sample", [P, KC, NS_])
        tables = mark[0]
        self.cos, self.sin = put("cos", [P, NT]), put("sin", [P, NT])
        shared = mark[0]
        mark[0] = tables
        self.ss, self.sq = put("ss", [P, 2, NH]), put("sq", [P, 2, NH])
        mark[0] = shared
        self.cqh, self.cql = split("cqn", [P, QC, NT])
        self.kvh, self.kvl = split("ckv", [P, CC, NT])
        self.keh, self.kel = split("kpe", [P, NT])
        after_latents = mark[0]
        self.qh, self.ql = split("q", [P, NT])
        self.peh, self.pel = split("q_pe", [P, NT])
        self.kh, self.kl = split("k", [P, NP_])
        self.vh, self.vl = split("v", [P, NP_])
        probs = mark[0]
        self.probs = put("probs", [P, PCOLS])
        self.pth, self.ptl = split("probs_t", [P, PCOLS])
        self.mx, self.nmx = put("mx", [P, KT]), put("nmx", [P, KT])
        self.rs, self.ri = put("rs", [P, KT]), put("ri", [P, KT])
        self.gb, self.ga = put("gb", [P, NT]), put("ga", [P, NT])
        self.cv = put("cv", [P, NT + 2])
        self.u = put("u", [P, NT + 4])
        self.ybt = put("ybt", [P, NP_])
        self.rope_t, self.rope_s = put("rope_t", [P, NH]), put("rope_s", [P, NH])
        mark[0] = after_latents
        self.cq = put("cq", [P, QC, NT])
        self.rk = put("rk", [P, 2, NT])
        self.ss1 = put("ss1", [P, 4, NH])
        assert mark[0] <= probs
        mark[0] = probs
        self.kv = put("kv", [P, CC, NT])
        self.kpe = put("kpe", [P, NT])
        self.sq1 = put("sq1", [P, 2, NH])
        self.rope1_t, self.rope1_s = put("rope1_t", [P, NH]), put("rope1_s", [P, NH])
        assert mark[0] <= probs + 3 * 4 * PCOLS
        mark[0] = shared
        self.cth, self.ctl, self.ctraw = split("cache_t", [P, CC, PAST], raw=True)
        self.kch, self.kcl, self.kcraw = split("cache_pe", [ROPE, PAST], raw=True)
        assert mark[0] <= shared + 2 * 4 * QC * NT
        mark[0] = after_latents
        self.nah, self.nal, self.naraw = split("cache_n", [P, 5, KL], raw=True)
        self.ps = put("probs_s", [P, NT])
        self.tsh, self.tsl = split("probs_s_t", [P, 5, P])
        self.och, self.ocl = split("context_s", [P, CC, P])
        self.ys = put("y_s", [P, 2, NS_])
        self.stat = put("stat_s", [P, 4])
        sample_end = mark[0]
        mark[0] = (top - 2 * 3 * 4096) // 32 * 32
        slots = mark[0]
        assert sample_end <= slots
        self.w8h, self.w8l, self.w8raw = split("w8", [P, 3, 1024], raw=True)
        mark[0] = shared
        self.fh, self.fl = split("f", [P, 2, 4, NT])
        self.ft, self.ff = put("ft", [P, 2, NH]), put("ff", [P, 2, NH])
        assert mark[0] <= slots

    def slot(self, s):
        if s < 5:
            return self.wh[:, s, :], self.wl[:, s, :], self.wraw[:, s, :]
        return self.w8h[:, s - 5, :], self.w8l[:, s - 5, :], self.w8raw[:, s - 5, :]

    def const(self, c, n=1):
        return self.consts[:, c:c + n]

    def gain(self, L, c, ahead=0):
        return self.consts[:, bass.ds(L * NG + (C_GAIN + ahead * NG + c), 1)]


def full(L, idx):
    return L * RING + (RING + idx + 1)


def may_fill(L, idx):
    return L * RING + (idx + 1)


def freed(L, idx):
    return L * RING + (idx + 5)


def w2_filled(L, g, k):
    return L * W2N + (W2N + 16 * g + k + 1)


def w2_may_fill(L, g, k):
    return L * W2N + (16 * g + k + 1)


def x_part(L, i):
    return L * 52 + (8 + i + 1)


X_NXB, X_WOA, X_WOB, X_WOS, X_FFA, X_FFB, X_NXA = 0, 8, 16, 24, 28, 36, 44


def square(L, i):
    return L * 74 + (8 + i + 1)


S_NXB, S_CQA, S_KVA0, S_CQB, S_KVB0, S_KVA1, S_KVB1 = 0, 8, 11, 12, 15, 16, 17
S_POSTA, S_MIX_O, S_PREB, S_FPA, S_MIX_2 = 18, 26, 42, 50, 58
MIX_O = [(1, 0), (0, 0), (0, 1), (1, 1), (0, 2), (0, 3), (1, 2), (0, 4), (0, 5), (1, 3), (0, 6), (0, 7),
         (1, 4), (1, 5), (1, 6), (1, 7)]
MIX_2 = [(1, 0), (1, 1), (1, 2), (1, 3), (0, 0), (1, 4), (0, 1), (1, 5), (0, 2), (1, 6), (0, 3), (1, 7),
         (0, 4), (0, 5), (0, 6), (0, 7)]


def root(L, e):
    return L * 12 + (e + 1)


def cols(s):
    return slice(NH * s, NH * (s + 1))


def mm3(pe, out, w, x, first, last):
    pe.matmul(out, w[1], x[0], start=first, stop=False)
    pe.matmul(out, w[0], x[1], start=False, stop=False)
    return pe.matmul(out, w[0], x[0], start=False, stop=last)


class Own:

    def __init__(self, dve, sem, base, steps):
        self.dve, self.sem, self.base, self.steps, self.n = dve, sem, base, steps, 0

    def step(self, ins):
        ins.then_inc(self.sem, 1)
        self.n += 1

    def wait(self, back=0):
        self.dve.wait_ge(self.sem, self.base + (self.n - back))

    def done(self):
        assert self.n == self.steps, (self.n, self.steps)


def program(nc, x_in, consts, tables, blocks, small, uv, cache_t, cache_n, cache_pe,
            x_out, kv_out, kpe_out, conv_out):
    with ExitStack() as ctx:
        pl = Plan(nc, ctx)
        block = ctx.enter_context(nc.Block())
        loads(nc, block, pl, x_in, consts, tables, blocks, small, uv, cache_t, cache_n, cache_pe, x_out)
        sums(nc, block, pl)
        scalar_engine(nc, block, pl, x_in, kv_out, kpe_out, conv_out)
        vector_engine(nc, block, pl)
        tensor_engine(nc, block, pl)


def loads(nc, block, pl, x_in, consts, tables, blocks, small, uv, cache_t, cache_n, cache_pe, x_out):

    @block.sync
    def _(sp):
        def slot_load(L, n, s):
            sp.dma_start(pl.slot(s)[2], blocks[L * NB + n]).then_inc(pl.slots[s], 16)

        sp.dma_start(pl.consts[:, :], consts).then_inc(pl.consts_landed, 16)
        for i in range(4):
            sp.dma_start(pl.x[:, 2 * i:2 * i + 2, cols(0)], x_in[:, 2 * i:2 * i + 2, cols(0)]) \
                .then_inc(pl.x_landed[i], 16)
            if i == 1:
                slot_load(0, 0, SLOT_P1[0])

        with sp.Fori(0, DEPTH) as L:
            for j in range(4):
                sp.wait_ge(pl.w2_full, L * W2N + 16 * (GROUPS - 1) + 8 + 2 * j + 1 + 1)
                slot_load(L, 1 + j, SLOT_P1[1 + j])
            sp.wait_ge(pl.s_valued, L * 4 + 1)
            sp.dma_start(pl.sraw[:, :], small[L * 5][:, 0:SWE]).then_inc(pl.small_landed, 16)
            sp.wait_ge(pl.ring_full, full(L, PRE_SUM[1]))
            sp.dma_start(pl.cos[:, :], tables[0]).then_inc(pl.tables_landed, 16)
            sp.dma_start(pl.sin[:, :], tables[1]).then_inc(pl.tables_landed, 16)
            sp.wait_ge(pl.ring_full, full(L, P1_B[0]))
            slot_load(L, 5, SLOT_P1[5])
            for i in range(N_HEAD):
                sp.wait_ge(pl.ring_full, full(L, P1_B[1 + i]))
                slot_load(L, n_head(0, i), SLOT_HD[i])
            with sp.Fori(0, HEADS // 2) as p:
                for e in range(2):
                    for i in range(N_HEAD):
                        if i == 2:
                            sp.wait_ge(pl.absorbed, L * HEADS + p * 2 + (e + 1))
                            if e == 0:
                                sp.dma_start(pl.sraw[:, 0:SWO], small[L * 5 + p][:, SWE:SWE + SWO]) \
                                    .then_inc(pl.small_landed, 16)
                            else:
                                sp.dma_start(pl.sraw[:, :], small[L * 5 + (p + 1)][:, 0:SWE]) \
                                    .then_inc(pl.small_landed, 16)
                        sp.wait_ge(pl.ring_full, L * RING + p * 20 + (RING + r_hd(e, i, 1) + 1))
                        sp.dma_start(pl.slot(SLOT_HD[i])[2], blocks[L * NB + p * 10 + (n_head(e + 1, i))]) \
                            .then_inc(pl.slots[SLOT_HD[i]], 16)
            sp.wait_ge(pl.projected, L * 40 + 40)
            sp.dma_start(pl.ctraw[:, :, :], cache_t[L]).then_inc(pl.cache_landed, 16)
            sp.dma_start(pl.kcraw[:, :], cache_pe[L]).then_inc(pl.cache_landed, 16)
            sp.wait_ge(pl.pv_made, L * HEADS + HEADS)
            sp.dma_start(pl.naraw[:, 0:4, :], cache_n[L]).then_inc(pl.nat_landed, 16)
            sp.wait_ge(pl.merged, L * HEADS + HEADS)
            for m in range(5, 8):
                slot_load(L, n_wo(m), SLOT_WO[m])
            sp.wait_ge(pl.s_valued, L * 4 + 3)
            sp.dma_start(pl.sraw[:, 0:1024], uv[L]).then_inc(pl.small_landed, 16)
            for j in range(4):
                sp.wait_ge(pl.ring_full, full(L, WO_B[SLOT_WO.index(SLOT_W1[j])]))
                slot_load(L, n_w1(0, j), SLOT_W1[j])
            for j in range(4):
                sp.wait_ge(pl.ring_full, full(L, r_w1(0, 1, j)))
                slot_load(L, n_w1(1, j), SLOT_W1[j])
            for j in range(4):
                slot_load(L, n_w2(0, j), SLOT_W2[j])
            with sp.Fori(0, GROUPS - 2) as g:
                for j in range(4):
                    sp.wait_ge(pl.ring_full, L * RING + g * 8 + (RING + r_w1(1, 1, j) + 1))
                    sp.dma_start(pl.slot(SLOT_W1[j])[2], blocks[L * NB + g * 8 + n_w1(2, j)]) \
                        .then_inc(pl.slots[SLOT_W1[j]], 16)
                for j in range(4):
                    sp.wait_ge(pl.w2_full, L * W2N + g * 16 + (W2N + 8 + 2 * j + 1 + 1))
                    sp.dma_start(pl.slot(SLOT_W2[j])[2], blocks[L * NB + g * 8 + n_w2(1, j)]) \
                        .then_inc(pl.slots[SLOT_W2[j]], 16)
            for j in range(4):
                sp.wait_ge(pl.ring_full, full(L, r_w1(GROUPS - 1, 1, j)))
                slot_load(L, n_w2(GROUPS - 1, j), SLOT_W1[j])
            sp.wait_ge(pl.w2_full, w2_filled(L, GROUPS - 2, 9))
            slot_load(L, NB, SLOT_P1[0])
        sp.wait_ge(pl.x_new, 32 * DEPTH)
        sp.dma_start(x_out[:, :, cols(0)], pl.x[:, :, cols(0)]).then_inc(pl.x_stored, 16)
        for m in range(0, KC, 2):
            sp.wait_ge(pl.x_new, 32 * DEPTH + m + 2)
            sp.dma_start(x_out[:, m:m + 2, cols(1)], pl.x[:, m:m + 2, cols(1)]).then_inc(pl.x_stored, 16)
        sp.wait_ge(pl.x_stored, 16 * (1 + KC // 2))


def sums(nc, block, pl):

    @block.gpsimd
    def _(pool):
        pool.sem_inc(pl.ring_full, RING)
        pool.sem_inc(pl.w2_full, W2N)
        pool.sem_inc(pl.ring_free, 4)
        pool.sem_inc(pl.w2_free, 4)
        pool.sem_inc(pl.summed, 2)
        pool.sem_inc(pl.s_valued, 1)
        pool.sem_inc(pl.pv_read, 1)

        def add(value, k, ss, sq, first):
            pool.wait_ge(pl.squared, value)
            pool.wait_ge(pl.summed, value + 1)
            if first:
                pool.sem_inc(pl.summed, 1)
            else:
                nc.gpsimd.tensor_tensor(ss, ss, sq[:, k % 2, :], ALU.add).then_inc(pl.summed, 1)

        def early_lo(L, i):
            hi, lo, raw = pl.slot(SLOT_P1[EARLY[i]])
            pool.wait_ge(pl.weights_hi, L * NB + (EARLY[i] + 1))
            nc.gpsimd.tensor_tensor(lo, raw, hi.bitcast(F32), ALU.subtract).then_inc(pl.early_lo, 1)

        def small_lo(value, n):
            pool.wait_ge(pl.small_hi, value)
            nc.gpsimd.tensor_tensor(pl.sl[:, 0:n], pl.sraw[:, 0:n], pl.sh[:, 0:n].bitcast(F32), ALU.subtract) \
                .then_inc(pl.small_lo, 1)

        for k in range(KC):
            add(k + 1, k, pl.ss[:, 0, :], pl.sq, k == 0)
        with pool.Fori(0, DEPTH) as L:
            early_lo(L, 0)
            early_lo(L, 1)
            for k in range(S_NXB, S_NXB + KC):
                add(square(L, k), k, pl.ss[:, 1, :], pl.sq, k == S_NXB)
                if k == S_NXB + 1:
                    early_lo(L, 2)
            for k, part in ((S_CQA, 0), (S_CQA + 1, 0), (S_CQA + 2, 0), (S_KVA0, 2),
                            (S_CQB, 1), (S_CQB + 1, 1), (S_CQB + 2, 1), (S_KVB0, 3), (S_KVA1, 2), (S_KVB1, 3)):
                add(square(L, k), k, pl.ss1[:, part, :], pl.sq1, k in (S_CQA, S_KVA0, S_CQB, S_KVB0))
            small_lo(L * 10 + 1, SWE)
            with pool.Fori(0, HEADS // 2) as p:
                small_lo(L * 10 + p * 2 + 2, SWO)
                small_lo(L * 10 + p * 2 + 3, SWE)
            def norm(at, mix):
                for k, (half, m) in enumerate(mix):
                    add(square(L, at + k), at + k, pl.ss[:, half, :], pl.sq, m == 0)

            norm(S_POSTA, [(0, m) for m in range(KC)])
            small_lo(L * 10 + 10, 1024)
            norm(S_MIX_O, MIX_O)
            norm(S_PREB, [(1, m) for m in range(KC)])
            norm(S_FPA, [(0, m) for m in range(KC)])
            norm(S_MIX_2, MIX_2)


def scalar_engine(nc, block, pl, x_in, kv_out, kpe_out, conv_out):
    act = nc.scalar

    @block.scalar
    def _(eng):
        def weight_hi(L, n, s, use):
            eng.wait_ge(pl.slots[s], (L * SLOT_USES[s] + use) * 16)
            hi, _, raw = pl.slot(s)
            act.activation(hi, raw, ACT.Copy).then_inc(pl.weights_hi, 1)

        def small_hi(L, j, n, more=0):
            eng.wait_ge(pl.small_landed, (L * 10 + (j + 1) + more) * 16)
            act.activation(pl.sh[:, 0:n], pl.sraw[:, 0:n], ACT.Copy).then_inc(pl.small_hi, 1)

        def square_of(src, L, k, sq, first=None):
            eng.wait_ge(pl.summed, square(L, k))
            out = sq[:, k % 2, :] if first is None else first
            act.activation(out, src, ACT.Square).then_inc(pl.squared, 1)

        def rooted(dst, L, idx, width):
            eng.wait_ge(pl.ring_full, full(L, idx))
            act.activation(dst, pl.ring[:, bank(idx), 0:NH], ACT.Sqrt, scale=1.0 / width,
                           bias=pl.const(C_EPS)).then_inc(pl.rooted, 1)

        def next_norm(L, m, half, col, x_new, part, k):
            cs = cols(half)
            eng.wait_ge(pl.x_new, x_new)
            apart()
            act.activation(pl.xh[:, m, cs], pl.x[:, m, cs], ACT.Copy, scale=col).then_inc(pl.x_hi, 1)
            square_of(pl.x[:, m, cs], L, k, pl.sq, pl.ss[:, half, :] if m == 0 else None)

        def apart():
            eng.sem_inc(pl.waits_apart, 1)

        def rope_halves(src, s_):
            for q in range(4):
                o = q ^ 1
                ins = act.activation(s_[32 * o:32 * o + 32, :], src[32 * q:32 * q + 32, :], ACT.Copy)
            ins.then_inc(pl.rope_swapped, 1)

        eng.wait_ge(pl.consts_landed, 16)
        cs = cols(0)
        for m in range(KC):
            if m % 2 == 0:
                eng.wait_ge(pl.x_landed[m // 2], 16)
            if m == 0:
                for i in range(4):
                    two = slice(2 * i, 2 * i + 2)
                    eng.dma_start(pl.x[:, two, cols(1)], x_in[:, two, cols(1)]).then_inc(pl.x_landed[4 + i], 16)
            act.activation(pl.xh[:, m, cs], pl.x[:, m, cs], ACT.Copy, scale=pl.const(C_GAIN + G_PRE + m)) \
                .then_inc(pl.x_hi, 1)
            eng.wait_ge(pl.summed, m + 1)
            out = pl.ss[:, 0, :] if m == 0 else pl.sq[:, m % 2, :]
            act.activation(out, pl.x[:, m, cs], ACT.Square).then_inc(pl.squared, 1)
            if m == 4:
                weight_hi(0, 0, SLOT_P1[0], use_p1(0))
        rooted(pl.rx2[:, cols(1)], 0, POST_SUM_B, D)

        with eng.Fori(0, DEPTH) as L:
            def latent_square(b, half, k):
                eng.wait_ge(pl.ring_free, freed(L, (P1_A, P1_B)[half][b]))
                src = pl.cq[:, b, cols(half)] if b < 3 else pl.kv[:, b - 3, cols(half)]
                part = {S_CQA: 0, S_CQB: 1, S_KVA0: 2, S_KVB0: 3}
                square_of(src, L, k, pl.sq1, pl.ss1[:, part[k], :] if k in part else None)

            for b in (1, 2):
                weight_hi(L, b, SLOT_P1[b], use_p1(b))
            for m in range(KC):
                next_norm(L, m, 1, pl.gain(L, G_PRE + m), L * 32 + m + 1, X_NXB + m, S_NXB + m)
                if m == 0:
                    rooted(pl.rx[:, cols(0)], L, PRE_SUM[0], D)
                    weight_hi(L, 3, SLOT_P1[3], use_p1(3))
            latent_square(0, 0, S_CQA)
            weight_hi(L, 4, SLOT_P1[4], use_p1(4))
            for b in range(1, 4):
                latent_square(b, 0, S_CQA + b)
            rooted(pl.rx[:, cols(1)], L, PRE_SUM[1], D)
            latent_square(0, 1, S_CQB)
            latent_square(1, 1, S_CQB + 1)
            weight_hi(L, 5, SLOT_P1[5], use_p1(5))
            latent_square(2, 1, S_CQB + 2)
            weight_hi(L, n_head(0, 0), SLOT_HD[0], use_hd(0, 0))
            latent_square(3, 1, S_KVB0)
            weight_hi(L, n_head(0, 1), SLOT_HD[1], use_hd(0, 1))
            latent_square(4, 0, S_KVA1)
            rooted(pl.rk[:, 0, cols(0)], L, P1_SUM[0], QL)
            weight_hi(L, n_head(0, 2), SLOT_HD[2], use_hd(0, 2))
            latent_square(4, 1, S_KVB1)
            rooted(pl.rk[:, 0, cols(1)], L, P1_SUM[1], QL)
            small_hi(L, 0, SWE)
            for half in range(2):
                eng.wait_ge(pl.ring_full, full(L, (P1_A, P1_B)[half][5]))
                rope_halves(pl.ring[:, bank((P1_A, P1_B)[half][5]), 0:NH], pl.rope1_s)
                rooted(pl.rk[:, 1, cols(half)], L, P1_SUM[2 + half], KL)

                def key_rope_hi():
                    eng.wait_ge(pl.rope_sum, L * 10 + half + 1)
                    act.activation(pl.keh[:, cols(half)], pl.kpe[:, cols(half)], ACT.Copy).then_inc(pl.rope_hi, 1)

                if half == 0:
                    key_rope_hi()
                src, hi, b0, n = ((pl.cq, pl.cqh, 0, QC), (pl.kv, pl.kvh, QC, CC))[half]
                for b in range(n):
                    eng.wait_ge(pl.latent_f, L * 5 + b0 + b + 1)
                    act.activation(hi[:, b, :], src[:, b, :], ACT.Copy).then_inc(pl.latent_hi, 1)
                if half == 1:
                    key_rope_hi()
            eng.dma_start(kpe_out[L], pl.kpe[0:ROPE, :]).then_inc(pl.latents_stored, 16)
            weight_hi(L, n_head(0, 3), SLOT_HD[3], use_hd(0, 3))
            act.activation(pl.kv_sample[:, :, :], pl.kv[:, :, NP_:NT], ACT.Copy).then_inc(pl.sample_kept, 1)
            eng.dma_start(kv_out[L], pl.kv[:, :, :]).then_inc(pl.latents_stored, 16)

            with eng.Fori(0, HEADS // 2) as p:
                for e in range(2):
                    def of_head(per_head, j):
                        return L * (HEADS * per_head) + p * (2 * per_head) + (e * per_head + j + 1)

                    def ring_freed(i, half):
                        return L * RING + p * 20 + (r_hd(e, i, half) + 5)

                    def next_weight(i):
                        h, i2 = (e, 4) if i == 0 else (e + 1, i - 1)
                        s = SLOT_HD[i2]
                        eng.wait_ge(pl.slots[s], L * (16 * SLOT_USES[s]) + p * 32 + 16 * use_hd(h, i2))
                        hi, _, raw = pl.slot(s)
                        act.activation(hi, raw, ACT.Copy).then_inc(pl.weights_hi, 1)

                    def projected(j):
                        eng.wait_ge(pl.projected, L * 40 + p * 10 + (6 * e + j + 1))

                    eng.wait_ge(pl.ring_free, ring_freed(0, 1))
                    act.activation(pl.gb[:, :], pl.gb[:, :], ACT.Tanh, scale=0.5).then_inc(pl.gated, 1)
                    for half in range(2):
                        projected(half)
                        act.activation(pl.qh[:, cols(half)], pl.att[:, 512 * half:512 * half + NH], ACT.Copy) \
                            .then_inc(pl.proj_hi, 1)
                    next_weight(0)
                    projected(2)
                    act.activation(pl.kh[:, :], pl.att[:, 1024:1536], ACT.Copy).then_inc(pl.proj_hi, 1)
                    projected(3)
                    act.activation(pl.vh[:, :], pl.att[:, 1536:2048], ACT.Copy).then_inc(pl.proj_hi, 1)
                    if e == 0:
                        for half in range(2):
                            projected(4 + half)
                            if half == 1:
                                eng.wait_ge(pl.rope_sum, L * 10 + p * 2 + 3)
                            rope_halves(pl.att[:, 512 * half:512 * half + NH], pl.rope_s)
                            eng.wait_ge(pl.rope_sum, L * 10 + p * 2 + (2 + half + 1))
                            act.activation(pl.peh[:, cols(half)], pl.rope_t[:, :], ACT.Copy).then_inc(pl.rope_hi, 1)
                        eng.wait_ge(pl.rope_lo, L * 10 + p * 2 + 4)
                        apart()
                        for hh in range(2):
                            rows = slice(64 * hh, 64 * hh + 64)
                            to = bass.ds(p * 128 + 64 * hh, 64)
                            act.activation(pl.qph[:, to], pl.peh[rows, NP_:NT].bitcast(F32), ACT.Copy) \
                                .then_inc(pl.pe_sample, 1)
                            act.activation(pl.qpl[:, to], pl.pel[rows, NP_:NT].bitcast(F32), ACT.Copy) \
                                .then_inc(pl.pe_sample, 1)
                    eng.wait_ge(pl.ring_free, ring_freed(1, 1))
                    act.activation(pl.ga[:, :], pl.ga[:, :], ACT.Tanh, scale=0.5).then_inc(pl.gated, 1)
                    next_weight(1)
                    eng.wait_ge(pl.absorbed, of_head(1, 0))
                    apart()
                    to = bass.ds(p * 128 + 64 * e, 64)
                    act.activation(pl.qah[:, :, to], pl.att[:, 1536:1664].rearrange("p (c q) -> p c q", c=2),
                                   ACT.Copy).then_inc(pl.abs_hi, 1)
                    if e == 0:
                        eng.wait_ge(pl.latents_stored, L * 32 + 32)
                    eng.wait_ge(pl.row_max, of_head(1, 0))
                    for t in range(KT):
                        act.activation(pl.probs[:, PO[t]:PO[t] + P * (t + 1)], score_tile(pl, t), ACT.Exp,
                                       scale=SCALE, bias=pl.nmx[:, t:t + 1], accum_out=pl.rs[:, t:t + 1]) \
                            .then_inc(pl.exped, 1)
                    next_weight(2)
                    eng.wait_ge(pl.small_landed, L * 160 + p * 32 + 16 * (e + 2))
                    n = SWO if e == 0 else SWE
                    act.activation(pl.sh[:, 0:n], pl.sraw[:, 0:n], ACT.Copy).then_inc(pl.small_hi, 1)
                    for k, (src, at, n) in enumerate(TURNED):
                        eng.wait_ge(pl.turned, of_head(3, k))
                        act.activation(pl.pth[:, at:at + n], pl.att[:, src:src + n], ACT.Copy) \
                            .then_inc(pl.turned_hi, 1)
                    eng.wait_ge(pl.ring_free, ring_freed(3, 1))
                    apart()
                    tail = pl.u[:, NP_:NP_ + 2 + 66].rearrange("p (a b) -> p a b", b=2)[:, 0:34:33, :]
                    act.activation(pl.conv_tail[:, p * 2 + e, :].rearrange("p (a b) -> p a b", b=2), tail, ACT.Copy)
                    act.activation(pl.cv[:, :], pl.u[:, 0:NT + 2], ACT.Copy,
                                   scale=conv_weight(pl, L, p, e, 0)).then_inc(pl.conv_first, 1)
                    next_weight(3)
                    next_weight(4)

            def x_hi_a(k):
                eng.wait_ge(pl.merged, L * HEADS + k + 1)
                act.activation(pl.xh[:, k, cols(0)], pl.my[:, k, cols(0)], ACT.Copy, scale=0.5).then_inc(pl.x_hi, 1)

            eng.wait_ge(pl.ring_full, full(L, r_hd(HEADS - 1, 4, 1)))
            for k in range(HEADS):
                x_hi_a(k)
            weight_hi(L, n_wo(4), SLOT_WO[4], use_wo(4))
            eng.dma_start(conv_out[L], pl.conv_tail[:, :, :]).then_inc(pl.conv_stored, 16)
            eng.wait_ge(pl.cache_landed, L * 32 + 32)
            act.activation(pl.cth[:, :, :], pl.ctraw[:, :, :], ACT.Copy).then_inc(pl.cache_hi, 1)
            act.activation(pl.kch[:, :], pl.kcraw[:, :], ACT.Copy).then_inc(pl.cache_hi, 1)
            eng.wait_ge(pl.nat_landed, L * 16 + 16)
            act.activation(pl.nah[:, 0:4, :], pl.naraw[:, 0:4, :], ACT.Copy).then_inc(pl.cache_hi, 1)
            eng.wait_ge(pl.new_turned, L + 1)
            act.activation(pl.nah[0:NS_, 4, :], pl.att[0:NS_, 1536:1792], ACT.Copy).then_inc(pl.cache_hi, 1)
            for k in range(HEADS):
                act.activation(pl.xh[:, k, NH:NP_], pl.my[:, k, NH:NP_], ACT.Copy, scale=0.5).then_inc(pl.x_hi, 1)

            def s_exp(t):
                eng.wait_ge(pl.s_max, L * 4 + t + 1)
                act.activation(pl.ps[:, :], pl.att[:, 0:NT], ACT.Exp, scale=SCALE, bias=pl.stat[:, 1:2],
                               accum_out=pl.stat[:, 2:3]).then_inc(pl.s_exped, 1)

            def s_turned_hi(t):
                eng.wait_ge(pl.s_turned, L * 4 + t + 1)
                act.activation(pl.tsh[:, 0:4, :], pl.att[:, 1024:1536].rearrange("p (k q) -> p k q", k=4), ACT.Copy)
                act.activation(pl.tsh[0:NS_, 4, :], pl.att[0:NS_, 576:704], ACT.Copy).then_inc(pl.s_thi, 1)

            def s_context_hi(t):
                eng.wait_ge(pl.s_context, L * 4 + t + 1)
                act.activation(pl.och[:, :, :], pl.att[:, 1664:1920].rearrange("p (c q) -> p c q", c=2), ACT.Copy) \
                    .then_inc(pl.s_chi, 1)

            def s_merged_hi(t):
                eng.wait_ge(pl.s_merged, L * 4 + t + 1)
                act.activation(pl.xh[:, 2 * t:2 * t + 2, NP_:NT], pl.my[:, 2 * t:2 * t + 2, NP_:NT], ACT.Copy,
                               scale=0.5).then_inc(pl.x_hi, 1)

            def post_square(ring_idx, m, half, k):
                eng.wait_ge(pl.ring_free, freed(L, ring_idx))
                square_of(pl.my[:, m, cols(half)], L, k, pl.sq, pl.ss[:, half, :] if m == 0 else None)

            s_exp(0)
            for m in range(4):
                post_square(WO_A[m], m, 0, S_POSTA + m)
            s_turned_hi(0)
            for t in (1, 2):
                for m in (0, 1):
                    if (t, m) != (2, 1):
                        weight_hi(L, n_wo(3 + 2 * t + m), 3 + 2 * t + m, use_wo(3 + 2 * t + m))
                    post_square(WO_A[2 * t + 2 + m], 2 * t + 2 + m, 0, S_POSTA + 2 * t + 2 + m)
                    if m == 0:
                        s_context_hi(t - 1)
                        s_exp(t)
                s_merged_hi(t - 1)
                s_turned_hi(t)
            s_context_hi(2)
            small_hi(L, 9, 1024)
            s_exp(3)
            rooted(pl.rx2[:, cols(0)], L, WO_SUM_A, D)
            s_merged_hi(2)
            s_turned_hi(3)
            s_context_hi(3)
            s_merged_hi(3)
            for k, (half, m) in enumerate(MIX_O):
                if half == 0:
                    next_norm(L, m, 0, pl.gain(L, G_FF + m), L * 32 + 8 + m + 1, X_FFA + m, S_MIX_O + k)
                else:
                    if m >= 4:
                        weight_hi(L, n_w1(0, m - 4), SLOT_W1[m - 4], use_w1(0, m - 4))
                    post_square(WO_B[m], m, 1, S_MIX_O + k)
            rooted(pl.rx[:, cols(0)], L, FF_SUM_A, D)

            def f_hi(ready, parity, half, j):
                eng.wait_ge(pl.f_made, ready)
                act.activation(pl.fh[:, parity, j, cols(half)], pl.ff[:, j % 2, :], ACT.Copy).then_inc(pl.f_hi, 1)

            def f_ready(g, k):
                return L * 64 + (8 * g + k + 1)

            f_hi(f_ready(0, 0), 0, 0, 0)
            rooted(pl.rx2[:, cols(1)], L, WO_SUM_B, D)
            for m in range(KC):
                next_norm(L, m, 1, pl.gain(L, G_FF + m), L * 32 + 16 + m + 1, X_FFB + m, S_PREB + m)
            for j in range(1, 4):
                f_hi(f_ready(0, j), 0, 0, j)
            rooted(pl.rx[:, cols(1)], L, FF_SUM_B, D)
            for j in range(4):
                f_hi(f_ready(0, 4 + j), 0, 1, j)
                if j >= 1:
                    weight_hi(L, n_w1(1, j - 1), SLOT_W1[j - 1], use_w1(1, j - 1))
            for k in range(8):
                f_hi(f_ready(1, k), 1, k // 4, k % 4)
                if k == 0:
                    weight_hi(L, n_w1(1, 3), SLOT_W1[3], use_w1(1, 3))
                elif 2 <= k < 6:
                    weight_hi(L, n_w2(0, k - 2), SLOT_W2[k - 2], use_w2(0, k - 2))

            def group_weight(g, j, which):
                s = (SLOT_W1, SLOT_W2)[which][j]
                use = (use_w1(2, j), use_w2(1, j))[which]
                eng.wait_ge(pl.slots[s], L * (16 * SLOT_USES[s]) + g * 16 + 16 * use)
                hi, _, raw = pl.slot(s)
                act.activation(hi, raw, ACT.Copy).then_inc(pl.weights_hi, 1)

            eng.wait_ge(pl.conv_stored, L * 16 + 16)
            for j in range(4):
                weight_hi(L, n_w1(2, j), SLOT_W1[j], use_w1(2, j))
            with eng.Fori(0, (GROUPS - 2) // 2) as i:
                for e in range(2):
                    for k in range(8):
                        f_hi(L * 64 + i * 16 + (8 * e + 16 + k + 1), e, k // 4, k % 4)
                        if k % 2 == 1:
                            group_weight(i * 2 + e, k // 2, 1)
                    for j in range(4):
                        group_weight(i * 2 + (e + 1), j, 0)
            weight_hi(L, NB, SLOT_P1[0], SLOT_USES[SLOT_P1[0]] + use_p1(0))
            for m in range(KC):
                eng.wait_ge(pl.w2_free, L * W2N + 16 * (GROUPS - 1) + m + 1 + 4)
                square_of(pl.my[:, m, cols(0)], L, S_FPA + m, pl.sq, pl.ss[:, 0, :] if m == 0 else None)
            for k, (half, m) in enumerate(MIX_2):
                if half == 0:
                    next_norm(L, m, 0, pl.gain(L, G_PRE + m, 1), L * 32 + 24 + m + 1, X_NXA + m, S_MIX_2 + k)
                else:
                    if m == 2:
                        rooted(pl.rx2[:, cols(0)], L, POST_SUM_A, D)
                    eng.wait_ge(pl.w2_free, L * W2N + 16 * (GROUPS - 1) + 8 + m + 1 + 4)
                    square_of(pl.my[:, m, cols(1)], L, S_MIX_2 + k, pl.sq, pl.ss[:, 1, :] if m == 0 else None)
                if (half, m) == (0, 5):
                    rooted(pl.rx2[:, cols(1)], L, NEXT_SUM_B, D)
        eng.wait_ge(pl.latents_stored, 32 * DEPTH)
        eng.wait_ge(pl.conv_stored, 16 * DEPTH)


TURNED = ((1536, PTO[0], 512), (0, PTO[1], 384), (512, PTO[2], 384))


def score_tile(pl, t):
    at = (0, 128, 512, 1024)[t]
    return pl.att[:, at:at + P * (t + 1)]


def conv_weight(pl, L, p, e, tap):
    return pl.consts[:, bass.ds(L * NG + p * 6 + (C_GAIN + G_CONV + 3 * e + tap), 1)]


def vector_engine(nc, block, pl):
    dve = nc.vector

    @block.vector
    def _(eng):
        def minus(out, a, hi):
            return dve.tensor_tensor(out, a, hi.bitcast(F32), ALU.subtract)

        def weight_lo(L, n, s):
            eng.wait_ge(pl.weights_hi, L * NB + (n + 1))
            hi, lo, raw = pl.slot(s)
            minus(lo, raw, hi).then_inc(pl.weights_lo, 1)

        def inverted(dst, L, idx, e):
            eng.wait_ge(pl.rooted, root(L, e))
            dve.reciprocal(dst, dst).then_inc(pl.ring_free, 1)

        dve.memset(pl.my[:, :, cols(1)], 0.0)
        dve.memset(pl.ss[:, 1, :], 1.0)
        eng.wait_ge(pl.consts_landed, 16)
        for m in range(KC):
            eng.wait_ge(pl.x_hi, m + 1)
            dve.scalar_tensor_tensor(out=pl.xl[:, m, cols(0)], in0=pl.x[:, m, cols(0)],
                                     scalar=pl.const(C_GAIN + G_PRE + m), in1=pl.xh[:, m, cols(0)].bitcast(F32),
                                     op0=ALU.mult, op1=ALU.subtract).then_inc(pl.x_lo, 1)
            if m == 5:
                weight_lo(0, 0, SLOT_P1[0])
        inverted(pl.rx2[:, cols(1)], 0, POST_SUM_B, 0)

        with eng.Fori(0, DEPTH) as L:
            def residual(half, idx, post, pre, part, between=None):
                cs = cols(half)
                eng.wait_ge(pl.ring_free, freed(L, idx))
                for m in range(KC + 2):
                    if m < KC:
                        own.step(dve.tensor_tensor(pl.my[:, m, cs], pl.my[:, m, cs], pl.rx2[:, cs], ALU.mult))
                    if 1 <= m <= KC:
                        own.wait(back=1 if m < KC else 0)
                        dve.scalar_tensor_tensor(out=pl.x[:, m - 1, cs], in0=pl.my[:, m - 1, cs],
                                                 scalar=post(m - 1), in1=pl.x[:, m - 1, cs],
                                                 op0=ALU.mult, op1=ALU.add).then_inc(pl.x_new, 1)
                    if m >= 2:
                        eng.wait_ge(pl.x_hi, x_part(L, part + m - 2))
                        dve.scalar_tensor_tensor(out=pl.xl[:, m - 2, cs], in0=pl.x[:, m - 2, cs], scalar=pre(m - 2),
                                                 in1=pl.xh[:, m - 2, cs].bitcast(F32), op0=ALU.mult,
                                                 op1=ALU.subtract).then_inc(pl.x_lo, 1)
                    if between:
                        between(m)

            own = Own(eng, pl.dve_own, L * OWN_L, OWN_1)

            def scaled_out(dst, idx, half):
                eng.wait_ge(pl.ring_full, full(L, idx))
                dve.tensor_tensor(dst, pl.ring[:, bank(idx), 0:NH], pl.rx[:, cols(half)], ALU.mult) \
                    .then_inc(pl.ring_free, 1)

            def latent(b, half):
                dst = pl.cq[:, b, cols(half)] if b < 3 else pl.kv[:, b - 3, cols(half)]
                scaled_out(dst, (P1_A, P1_B)[half][b], half)

            def first_latent(half):
                rx = pl.rx[:, cols(half)]
                eng.wait_ge(pl.rooted, root(L, 1 + half))
                own.step(dve.reciprocal(rx, rx))
                own.wait()
                latent(0, half)
                dve.tensor_tensor(pl.rx2[:, cols(half)], rx, rx, ALU.mult).then_inc(pl.ring_free, 1)

            for i in range(4):
                eng.wait_ge(pl.x_landed[4 + i], 16)

            def latents_between(m):
                if m == 1:
                    first_latent(0)
                if m == 7:
                    latent(1, 0)

            residual(1, POST_SUM_B, lambda m: pl.gain(L, G_FPOST + m, -1), lambda m: pl.gain(L, G_PRE + m), X_NXB,
                     latents_between)
            eng.sem_inc(pl.weights_lo, len(EARLY))
            weight_lo(L, 4, SLOT_P1[4])
            for b in range(2, 4):
                latent(b, 0)
            first_latent(1)
            latent(1, 1)
            weight_lo(L, 5, SLOT_P1[5])
            latent(2, 1)
            weight_lo(L, n_head(0, 0), SLOT_HD[0])
            latent(3, 1)
            weight_lo(L, n_head(0, 1), SLOT_HD[1])
            latent(4, 0)
            inverted(pl.rk[:, 0, cols(0)], L, P1_SUM[0], 3)
            weight_lo(L, n_head(0, 2), SLOT_HD[2])
            latent(4, 1)
            inverted(pl.rk[:, 0, cols(1)], L, P1_SUM[1], 4)
            eng.wait_ge(pl.tables_landed, L * 32 + 32)
            for half in range(2):
                cs, idx = cols(half), (P1_A, P1_B)[half][5]
                eng.wait_ge(pl.ring_full, full(L, idx))
                eng.wait_ge(pl.rope_swapped, L * 10 + half + 1)
                own.step(dve.tensor_tensor(pl.rope1_t[:, :], pl.ring[:, bank(idx), 0:NH], pl.cos[:, cs], ALU.mult))
                dve.tensor_tensor(pl.rope1_s[:, :], pl.rope1_s[:, :], pl.sin[:, cs], ALU.mult) \
                    .then_inc(pl.ring_free, 1)
                eng.wait_ge(pl.ring_free, freed(L, idx))

                def key_rope_end():
                    own.step(dve.tensor_tensor(pl.rope1_t[:, :], pl.rope1_t[:, :], pl.rope1_s[:, :], ALU.add))
                    own.wait()
                    dve.tensor_tensor(pl.kpe[:, cs], pl.rope1_t[:, :], pl.rx[:, cs], ALU.mult) \
                        .then_inc(pl.rope_sum, 1)

                def key_rope_lo():
                    eng.wait_ge(pl.rope_hi, L * 10 + half + 1)
                    minus(pl.kel[:, cs], pl.kpe[:, cs], pl.keh[:, cs]).then_inc(pl.rope_lo, 1)

                if half == 0:
                    key_rope_end()
                    for b in range(QC):
                        dve.scalar_tensor_tensor(out=pl.cq[:, b, :], in0=pl.cq[:, b, :],
                                                 scalar=pl.gain(L, G_Q + b), in1=pl.rk[:, 0, :],
                                                 op0=ALU.mult, op1=ALU.mult).then_inc(pl.latent_f, 1)
                    inverted(pl.rk[:, 1, cs], L, P1_SUM[2], 5)
                    key_rope_lo()
                    for b in range(QC):
                        eng.wait_ge(pl.latent_hi, L * 5 + b + 1)
                        minus(pl.cql[:, b, :], pl.cq[:, b, :], pl.cqh[:, b, :]).then_inc(pl.latent_lo, 1)
                else:
                    inverted(pl.rk[:, 1, cs], L, P1_SUM[3], 6)
                    eng.wait_ge(pl.ring_free, freed(L, P1_SUM[3]))
                    for c in range(CC):
                        dve.scalar_tensor_tensor(out=pl.kv[:, c, :], in0=pl.kv[:, c, :],
                                                 scalar=pl.gain(L, G_KV + c), in1=pl.rk[:, 1, :],
                                                 op0=ALU.mult, op1=ALU.mult).then_inc(pl.latent_f, 1)
                    for c in range(CC):
                        eng.wait_ge(pl.latent_hi, L * 5 + QC + c + 1)
                        minus(pl.kvl[:, c, :], pl.kv[:, c, :], pl.kvh[:, c, :]).then_inc(pl.latent_lo, 1)
                    key_rope_end()
                    key_rope_lo()
            weight_lo(L, n_head(0, 3), SLOT_HD[3])
            own.done()

            with eng.Fori(0, HEADS // 2) as p:
                own = Own(eng, pl.dve_own, L * OWN_L + p * OWN_PAIR + OWN_1, OWN_PAIR)
                for e in range(2):
                    def of_head(per_head, j):
                        return L * (HEADS * per_head) + p * (2 * per_head) + (e * per_head + j + 1)

                    def ring_value(i, half, more):
                        return L * RING + p * 20 + (r_hd(e, i, half) + 1 + more)

                    def entry(i, half):
                        eng.wait_ge(pl.ring_full, ring_value(i, half, RING))
                        return pl.ring[:, bank(r_hd(e, i, half)), 0:NH]

                    def head_out(dst, i, half, factor):
                        src = entry(i, half)
                        dve.tensor_tensor(dst, src, factor[:, cols(half)], ALU.mult).then_inc(pl.ring_free, 1)

                    def own_ring(i, half):
                        eng.wait_ge(pl.ring_free, ring_value(i, half, 4))

                    def next_weight(i):
                        n = n_head(e, 4) if i == 0 else n_head(e + 1, i - 1)
                        eng.wait_ge(pl.weights_hi, L * NB + p * 10 + (n + 1))
                        hi, lo, raw = pl.slot(SLOT_HD[4 if i == 0 else i - 1])
                        minus(lo, raw, hi).then_inc(pl.weights_lo, 1)

                    def proj_lo(j, lo, src, hi):
                        eng.wait_ge(pl.proj_hi, of_head(4, j))
                        minus(lo, src, hi).then_inc(pl.proj_lo, 1)

                    head_out(pl.gb[:, cols(0)], 0, 0, pl.rx)
                    head_out(pl.gb[:, cols(1)], 0, 1, pl.rx)
                    for half in range(2):
                        proj_lo(half, pl.ql[:, cols(half)], pl.att[:, 512 * half:512 * half + NH],
                                pl.qh[:, cols(half)])
                    next_weight(0)
                    proj_lo(2, pl.kl[:, :], pl.att[:, 1024:1536], pl.kh[:, :])
                    proj_lo(3, pl.vl[:, :], pl.att[:, 1536:2048], pl.vh[:, :])
                    if e == 0:
                        for half in range(2):
                            cs, src = cols(half), pl.att[:, 512 * half:512 * half + NH]
                            eng.wait_ge(pl.projected, L * 40 + p * 10 + (4 + half + 1))
                            if half == 1:
                                eng.wait_ge(pl.rope_lo, L * 10 + p * 2 + 3)
                            eng.wait_ge(pl.rope_swapped, L * 10 + p * 2 + (2 + half + 1))
                            own.step(dve.tensor_tensor(pl.rope_t[:, :], src, pl.cos[:, cs], ALU.mult))
                            own.step(dve.tensor_tensor(pl.rope_s[:, :], pl.rope_s[:, :], pl.sin[:, cs], ALU.mult))
                            own.wait()
                            dve.tensor_tensor(pl.rope_t[:, :], pl.rope_t[:, :], pl.rope_s[:, :], ALU.add) \
                                .then_inc(pl.rope_sum, 1)
                            eng.wait_ge(pl.rope_hi, L * 10 + p * 2 + (2 + half + 1))
                            minus(pl.pel[:, cs], pl.rope_t[:, :], pl.peh[:, cs]).then_inc(pl.rope_lo, 1)
                    head_out(pl.ga[:, cols(0)], 1, 0, pl.rx)
                    head_out(pl.ga[:, cols(1)], 1, 1, pl.rx)
                    next_weight(1)
                    eng.wait_ge(pl.abs_hi, of_head(1, 0))
                    to = bass.ds(p * 128 + 64 * e, 64)
                    dve.tensor_tensor(pl.qal[:, :, to], pl.att[:, 1536:1664].rearrange("p (c q) -> p c q", c=2),
                                      pl.qah[:, :, to].bitcast(F32), ALU.subtract).then_inc(pl.abs_lo, 1)
                    for t in range(KT):
                        eng.wait_ge(pl.scored, of_head(4, max(t, 1)))
                        own.step(dve.memset(score_tile(pl, t)[0:CH, P * (t + 1) - CH:P * (t + 1)], NEG))
                    for t in range(KT):
                        own.wait(back=KT - 1)
                        own.step(dve.tensor_reduce(pl.mx[:, t:t + 1], score_tile(pl, t), AXX, ALU.max))
                    own.wait()
                    dve.tensor_scalar(pl.nmx[:, :], pl.mx[:, :], -SCALE, None, ALU.mult).then_inc(pl.row_max, 1)
                    head_out(pl.cv[:, cols(0)], 2, 0, pl.rx2)
                    eng.wait_ge(pl.exped, of_head(4, KT - 1))
                    own.step(dve.reciprocal(pl.ri[:, :], pl.rs[:, :]))
                    own.wait()
                    for t in range(KT):
                        tile = pl.probs[:, PO[t]:PO[t] + P * (t + 1)]
                        dve.tensor_scalar(tile, tile, pl.ri[:, t:t + 1], None, ALU.mult).then_inc(pl.normed, 1)
                    head_out(pl.cv[:, cols(1)], 2, 1, pl.rx2)
                    next_weight(2)
                    for k, (src, at, n) in enumerate(TURNED):
                        eng.wait_ge(pl.turned_hi, of_head(3, k))
                        minus(pl.ptl[:, at:at + n], pl.att[:, src:src + n], pl.pth[:, at:at + n]) \
                            .then_inc(pl.turned_lo, 1)
                    dve.memset(pl.u[:, 0:2], 0.0)
                    dve.tensor_copy(pl.u[:, 2 + NP_:4 + NP_],
                                    pl.consts[:, bass.ds(L * (2 * KC) + p * 4 + (C_STATE + 2 * e), 2)])
                    own_ring(2, 1)
                    src = entry(3, 0)
                    dve.tensor_tensor(pl.u[:, 2:2 + NH], src, pl.cv[:, 0:NH], ALU.mult).then_inc(pl.ring_free, 1)
                    src = entry(3, 1)
                    dve.tensor_tensor(pl.u[:, 2 + NH:2 + NP_], src[:, 0:NP_ - NH], pl.cv[:, NH:NP_], ALU.mult)
                    dve.tensor_tensor(pl.u[:, 4 + NP_:4 + NT], src[:, NP_ - NH:NH], pl.cv[:, NP_:NT], ALU.mult) \
                        .then_inc(pl.ring_free, 1)
                    next_weight(3)
                    eng.wait_ge(pl.conv_first, of_head(1, 0))
                    for tap in (1, 2):
                        own.step(dve.scalar_tensor_tensor(out=pl.cv[:, :], in0=pl.u[:, tap:tap + NT + 2],
                                                          scalar=conv_weight(pl, L, p, e, tap), in1=pl.cv[:, :],
                                                          op0=ALU.mult, op1=ALU.add))
                        own.wait()
                    dve.scalar_tensor_tensor(out=pl.ga[:, 0:NP_], in0=pl.ga[:, 0:NP_], scalar=1.0,
                                             in1=pl.cv[:, 0:NP_], op0=ALU.add, op1=ALU.mult)
                    own.step(dve.scalar_tensor_tensor(out=pl.ga[:, NP_:NT], in0=pl.ga[:, NP_:NT], scalar=1.0,
                                                      in1=pl.cv[:, NP_ + 2:NT + 2], op0=ALU.add, op1=ALU.mult))
                    own.wait()
                    own.step(dve.tensor_tensor(pl.ga[:, :], pl.ga[:, :], pl.rx[:, :], ALU.mult))
                    next_weight(4)
                    eng.wait_ge(pl.pv_made, of_head(1, 0))
                    dve.tensor_scalar(pl.sgb[:, p * 2 + e, :], pl.gb[:, NP_:NT], 1.0, None, ALU.add)
                    dve.scalar_tensor_tensor(out=pl.ybt[:, :], in0=pl.gb[:, 0:NP_], scalar=1.0,
                                             in1=pl.att[:, 1024:1536], op0=ALU.add, op1=ALU.mult) \
                        .then_inc(pl.pv_read, 1)
                    own.wait()
                    for half in range(2):
                        src = entry(4, half)
                        dve.tensor_tensor(pl.my[:, p * 2 + e, cols(half)], src, pl.ga[:, cols(half)], ALU.mult) \
                            .then_inc(pl.ring_free, 1)
                    own_ring(4, 1)
                    dve.tensor_tensor(pl.my[:, p * 2 + e, 0:NP_], pl.my[:, p * 2 + e, 0:NP_], pl.ybt[:, :], ALU.add) \
                        .then_inc(pl.merged, 1)
                own.done()

            own = Own(eng, pl.dve_own, L * OWN_L + OWN_1 + OWN_PAIR * HEADS // 2, OWN_3)

            def merged_lo(i, m, t):
                eng.wait_ge(pl.x_hi, x_part(L, i))
                dve.scalar_tensor_tensor(out=pl.xl[:, m, t], in0=pl.my[:, m, t], scalar=0.5,
                                         in1=pl.xh[:, m, t].bitcast(F32), op0=ALU.mult, op1=ALU.subtract) \
                    .then_inc(pl.x_lo, 1)

            def cache_lo(i, lo, src, hi):
                eng.wait_ge(pl.cache_hi, L * 4 + i + 1)
                minus(lo, src, hi).then_inc(pl.cache_lo, 1)

            for k in range(HEADS):
                merged_lo(X_WOA + k, k, cols(0))
            weight_lo(L, n_wo(4), SLOT_WO[4])
            cache_lo(0, pl.ctl[:, :, :], pl.ctraw[:, :, :], pl.cth[:, :, :])
            cache_lo(1, pl.kcl[:, :], pl.kcraw[:, :], pl.kch[:, :])
            cache_lo(2, pl.nal[:, 0:4, :], pl.naraw[:, 0:4, :], pl.nah[:, 0:4, :])
            cache_lo(3, pl.nal[0:NS_, 4, :], pl.att[0:NS_, 1536:1792], pl.nah[0:NS_, 4, :])
            for k in range(HEADS):
                merged_lo(X_WOB + k, k, slice(NH, NP_))

            def s_max(t):
                eng.wait_ge(pl.s_scored, L * 4 + t + 1)
                own.step(dve.tensor_reduce(pl.stat[:, 0:1], pl.att[:, 0:NT], AXX, ALU.max))
                own.wait()
                dve.tensor_scalar(pl.stat[:, 1:2], pl.stat[:, 0:1], -SCALE, None, ALU.mult).then_inc(pl.s_max, 1)

            def s_normed(t):
                eng.wait_ge(pl.s_exped, L * 4 + t + 1)
                own.step(dve.reciprocal(pl.stat[:, 3:4], pl.stat[:, 2:3]))
                own.wait()
                dve.tensor_scalar(pl.ps[:, :], pl.ps[:, :], pl.stat[:, 3:4], None, ALU.mult).then_inc(pl.s_normed, 1)

            def s_turned_lo(t):
                eng.wait_ge(pl.s_thi, L * 4 + t + 1)
                minus(pl.tsl[:, 0:4, :], pl.att[:, 1024:1536].rearrange("p (k q) -> p k q", k=4), pl.tsh[:, 0:4, :])
                minus(pl.tsl[0:NS_, 4, :], pl.att[0:NS_, 576:704], pl.tsh[0:NS_, 4, :]).then_inc(pl.s_tlo, 1)

            def s_context_lo(t):
                eng.wait_ge(pl.s_chi, L * 4 + t + 1)
                minus(pl.ocl[:, :, :], pl.att[:, 1664:1920].rearrange("p (c q) -> p c q", c=2), pl.och[:, :, :]) \
                    .then_inc(pl.s_clo, 1)

            def s_merged(t):
                eng.wait_ge(pl.s_valued, L * 4 + t + 2)
                two = slice(2 * t, 2 * t + 2)
                own.step(dve.tensor_tensor(pl.ys[:, :, :], pl.att[:, 1920:2048].rearrange("p (h q) -> p h q", h=2),
                                           pl.sgb[:, two, :], ALU.mult))
                own.wait()
                dve.tensor_tensor(pl.my[:, two, NP_:NT], pl.my[:, two, NP_:NT], pl.ys[:, :, :], ALU.add) \
                    .then_inc(pl.s_merged, 1)
                merged_lo(X_WOS + t, two, slice(NP_, NT))

            def wo_out(idx, m, half):
                eng.wait_ge(pl.ring_full, full(L, idx))
                dve.tensor_copy(pl.my[:, m, cols(half)], pl.ring[:, bank(idx), 0:NH]).then_inc(pl.ring_free, 1)

            s_max(0)
            wo_out(WO_A[0], 0, 0)
            wo_out(WO_A[1], 1, 0)
            s_normed(0)
            wo_out(WO_A[2], 2, 0)
            wo_out(WO_A[3], 3, 0)
            s_turned_lo(0)
            for t in (1, 2):
                for m in (0, 1):
                    wo_out(WO_A[2 * t + 2 + m], 2 * t + 2 + m, 0)
                    if (t, m) != (2, 1):
                        weight_lo(L, n_wo(3 + 2 * t + m), 3 + 2 * t + m)
                    if m == 0:
                        s_context_lo(t - 1)
                        s_max(t)
                        s_normed(t)
                s_merged(t - 1)
                s_turned_lo(t)
            s_context_lo(2)
            s_max(3)
            s_normed(3)
            inverted(pl.rx2[:, cols(0)], L, WO_SUM_A, 7)
            s_merged(2)
            s_turned_lo(3)
            s_context_lo(3)
            s_merged(3)
            ffn_gain = lambda m: pl.gain(L, G_FF + m)
            post_gain = lambda m: pl.gain(L, G_POST + m)

            wo_out(WO_B[0], 0, 1)
            residual(0, WO_SUM_A, post_gain, ffn_gain, X_FFA,
                     between=lambda m: wo_out(WO_B[m // 2], m // 2, 1) if m in (2, 4, 6) else None)
            for m in range(4, 8):
                wo_out(WO_B[m], m, 1)
                weight_lo(L, n_w1(0, m - 4), SLOT_W1[m - 4])
            inverted(pl.rx[:, cols(0)], L, FF_SUM_A, 8)
            own.done()

            own = Own(eng, pl.dve_own, L * OWN_L + OWN_1 + OWN_PAIR * HEADS // 2 + OWN_3, OWN_4)

            def hidden(ring_end, made, idx, parity, half, j, after=False):
                eng.wait_ge(pl.ring_full, ring_end + RING)
                dve.tensor_tensor(pl.ft[:, j % 2, :], pl.ring[:, bank(idx), 0:NH], pl.rx[:, cols(half)], ALU.mult) \
                    .then_inc(pl.ring_free, 1)
                eng.wait_ge(pl.ring_free, ring_end + 4)
                if after:
                    eng.sem_inc(pl.ring_free, 1)
                dve.scalar_tensor_tensor(out=pl.ff[:, j % 2, :], in0=pl.ft[:, j % 2, :], scalar=0.0,
                                         in1=pl.ft[:, j % 2, :], op0=ALU.max, op1=ALU.mult).then_inc(pl.f_made, 1)
                eng.wait_ge(pl.f_hi, made)
                minus(pl.fl[:, parity, j, cols(half)], pl.ff[:, j % 2, :], pl.fh[:, parity, j, cols(half)]) \
                    .then_inc(pl.f_lo, 1)

            def hidden_of(g, half, j, after=False):
                idx = r_w1(g, half, j)
                hidden(L * RING + (idx + 1), L * 64 + (8 * g + 4 * half + j + 1), idx, g % 2, half, j,
                       after)

            def w2_out(value, k, first=False):
                m, half = k % 8, k // 8
                eng.wait_ge(pl.w2_full, value)
                src, dst = pl.att[:, 512 * (k % 4):512 * (k % 4) + NH], pl.my[:, m, cols(half)]
                if first:
                    dve.tensor_copy(dst, src).then_inc(pl.w2_free, 1)
                else:
                    dve.tensor_tensor(dst, dst, src, ALU.add).then_inc(pl.w2_free, 1)

            eng.wait_ge(pl.ring_free, freed(L, FF_SUM_A))
            hidden_of(0, 0, 0)
            inverted(pl.rx2[:, cols(1)], L, WO_SUM_B, 9)
            residual(1, WO_SUM_B, post_gain, ffn_gain, X_FFB)
            for j in range(1, 4):
                hidden_of(0, 0, j)
            rx = pl.rx[:, cols(1)]
            eng.wait_ge(pl.rooted, root(L, 10))
            own.step(dve.reciprocal(rx, rx))
            own.wait()
            hidden_of(0, 1, 0, after=True)
            for j in range(1, 4):
                hidden_of(0, 1, j)
                weight_lo(L, n_w1(1, j - 1), SLOT_W1[j - 1])
            for k in range(8):
                hidden_of(1, k // 4, k % 4)
                if k == 0:
                    weight_lo(L, n_w1(1, 3), SLOT_W1[3])
                elif 2 <= k < 6:
                    weight_lo(L, n_w2(0, k - 2), SLOT_W2[k - 2])

            def group_weight(g, j, which):
                n = (n_w1(2, j), n_w2(1, j))[which]
                eng.wait_ge(pl.weights_hi, L * NB + g * 8 + (n + 1))
                hi, lo, raw = pl.slot((SLOT_W1, SLOT_W2)[which][j])
                minus(lo, raw, hi).then_inc(pl.weights_lo, 1)

            for k in range(16):
                w2_out(w2_filled(L, 0, k), k, first=True)
                if k % 4 == 2:
                    j = k // 4
                    weight_lo(L, n_w1(2, j), SLOT_W1[j])
            with eng.Fori(0, (GROUPS - 2) // 2) as i:
                for e in range(2):
                    for k in range(8):
                        idx = r_w1(2 + e, k // 4, k % 4)
                        hidden(L * RING + i * 16 + (idx + 1), L * 64 + i * 16 + (8 * (e + 2) + k + 1),
                               idx, e, k // 4, k % 4)
                        if k % 2 == 1:
                            group_weight(i * 2 + e, k // 2, 1)
                    for k in range(16):
                        w2_out(L * W2N + i * 32 + (W2N + 16 * (e + 1) + k + 1), k)
                        if k % 4 == 2:
                            group_weight(i * 2 + (e + 1), k // 4, 0)
            weight_lo(L, NB, SLOT_P1[0])
            g = GROUPS - 1
            next_gain = lambda m: pl.gain(L, G_PRE + m, 1)
            ffn_post_gain = lambda m: pl.gain(L, G_FPOST + m)
            for k in range(8):
                w2_out(w2_filled(L, g, k), k)
            for k in (8, 9):
                w2_out(w2_filled(L, g, k), k)
            inverted(pl.rx2[:, cols(0)], L, POST_SUM_A, 11)
            for k in (10, 11):
                w2_out(w2_filled(L, g, k), k)
            residual(0, POST_SUM_A, ffn_post_gain, next_gain, X_NXA,
                     between=lambda m: w2_out(w2_filled(L, g, 11 + m), 11 + m) if 1 <= m <= 4 else None)
            inverted(pl.rx2[:, cols(1)], L, NEXT_SUM_B, 12)
            own.done()
        own = Own(eng, pl.dve_own, DEPTH * OWN_L, KC)
        eng.wait_ge(pl.ring_free, freed(DEPTH, POST_SUM_B))
        for m in range(KC + 1):
            if m < KC:
                own.step(dve.tensor_tensor(pl.my[:, m, cols(1)], pl.my[:, m, cols(1)], pl.rx2[:, cols(1)], ALU.mult))
            if m >= 1:
                own.wait(back=1 if m < KC else 0)
                dve.scalar_tensor_tensor(out=pl.x[:, m - 1, cols(1)], in0=pl.my[:, m - 1, cols(1)],
                                         scalar=pl.const(C_GAIN + (DEPTH - 1) * NG + G_FPOST + m - 1),
                                         in1=pl.x[:, m - 1, cols(1)], op0=ALU.mult, op1=ALU.add) \
                    .then_inc(pl.x_new, 1)
        own.done()


def tensor_engine(nc, block, pl):
    pe = nc.tensor
    ones, ident = pl.const(C_ONE, P), pl.const(C_ID, P)
    att = pl.att

    def rows_of(pair, *at):
        return pair[0][at], pair[1][at]

    xs, small = (pl.xh, pl.xl), (pl.sh, pl.sl)
    cqn, ckv, kpe = (pl.cqh, pl.cql), (pl.kvh, pl.kvl), (pl.keh, pl.kel)
    q, q_pe, k_, v = (pl.qh, pl.ql), (pl.peh, pl.pel), (pl.kh, pl.kl), (pl.vh, pl.vl)
    probs_t = (pl.pth, pl.ptl)
    q_abs, q_pe_sample = (pl.qah, pl.qal), (pl.qph, pl.qpl)
    cache_t, cache_pe, cache_n = (pl.cth, pl.ctl), (pl.kch, pl.kcl), (pl.nah, pl.nal)
    probs_s_t, context, f = (pl.tsh, pl.tsl), (pl.och, pl.ocl), (pl.fh, pl.fl)
    ALL = slice(0, P)

    @block.tensor
    def _(eng):
        def norm_sum(L, idx, ss, k):
            eng.wait_ge(pl.ring_free, may_fill(L, idx))
            eng.wait_ge(pl.summed, square(L, k) + 2)
            pe.matmul(pl.ring[:, bank(idx), 0:NH], ones, ss, start=True, stop=True).then_inc(pl.ring_full, 1)

        eng.wait_ge(pl.x_lo, 1)
        norm_sum(0, POST_SUM_B, pl.ss[:, 1, :], -KC)
        with eng.Fori(0, DEPTH) as L:
            def block_half(L_ring, idx, s, half, weight=None, x_ready=None, k0=0, k1=KC):
                if k0 == 0:
                    eng.wait_ge(pl.ring_free, L_ring + (idx + 1))
                if weight is not None:
                    eng.wait_ge(pl.weights_lo, weight)
                hi, lo, _ = pl.slot(s)
                out = pl.ring[:, bank(idx), 0:NH]
                for k in range(k0, k1):
                    if x_ready:
                        eng.wait_ge(pl.x_lo, x_ready(k))
                    w = slice(k * P, (k + 1) * P)
                    last = mm3(pe, out, (hi[:, w], lo[:, w]), rows_of(xs, ALL, k, cols(half)), k == 0, k == KC - 1)
                if k1 == KC:
                    last.then_inc(pl.ring_full, 1)

            def latent_block(b, half):
                ready = (lambda k: L * 52 + (8 * half + k + 1)) if b == 0 else None
                if half == 0 and b in EARLY:
                    eng.wait_ge(pl.early_lo, L * len(EARLY) + b)
                weight = L * NB + (b + 1) if b not in EARLY else None
                block_half(L * RING, (P1_A, P1_B)[half][b], SLOT_P1[b], half, weight, ready)

            for half in range(2):
                latent_block(0, half)
                norm_sum(L, PRE_SUM[half], pl.ss[:, half, :], S_NXB + 8 * half - 1)
                for b in range(1, 4):
                    latent_block(b, half)
            latent_block(4, 0)
            norm_sum(L, P1_SUM[0], pl.ss1[:, 0, :], S_CQA + 2)
            latent_block(4, 1)
            norm_sum(L, P1_SUM[1], pl.ss1[:, 1, :], S_CQB + 2)
            latent_block(5, 0)
            norm_sum(L, P1_SUM[2], pl.ss1[:, 2, :], S_KVA1)
            latent_block(5, 1)
            norm_sum(L, P1_SUM[3], pl.ss1[:, 3, :], S_KVB1)

            with eng.Fori(0, HEADS // 2) as p:
                for e in range(2):
                    def of_head(per_head, j):
                        return L * (HEADS * per_head) + p * (2 * per_head) + (e * per_head + j + 1)

                    def head_block(i):
                        for half in range(2):
                            block_half(L * RING + p * 20, r_hd(e, i, half), SLOT_HD[i], half,
                                       L * NB + p * 10 + (n_head(e, i) + 1) if half == 0 else None)

                    def small_w(at, c):
                        return rows_of(small, ALL, slice(at + c * P, at + (c + 1) * P))

                    def query(at, half):
                        out = att[:, 512 * half:512 * half + NH]
                        for k in range(QC):
                            last = mm3(pe, out, small_w(at, k), rows_of(cqn, ALL, k, cols(half)), k == 0, k == QC - 1)
                        last.then_inc(pl.projected, 1)

                    head_block(0)
                    eng.wait_ge(pl.small_lo, L * 10 + p * 2 + (e + 1))
                    eng.wait_ge(pl.latent_lo, L * 5 + QC)
                    query(UQ, 0)
                    query(UQ, 1)
                    eng.wait_ge(pl.latent_lo, L * 5 + QC + CC)
                    eng.wait_ge(pl.pv_read, L * HEADS + p * 2 + (e + 1))
                    for c in range(CC):
                        last = mm3(pe, att[:, 1024:1536], small_w(UK, c), rows_of(ckv, ALL, c, slice(0, NP_)),
                                   c == 0, c == CC - 1)
                    last.then_inc(pl.projected, 1)
                    for kt in range(KT):
                        keys = slice(P * kt, P * (kt + 1))
                        for c in range(CC):
                            last = mm3(pe, att[:, 1536 + P * kt:1536 + P * (kt + 1)], rows_of(ckv, ALL, c, keys),
                                       small_w(UV, c), c == 0, c == CC - 1)
                    last.then_inc(pl.projected, 1)
                    if e == 0:
                        eng.wait_ge(pl.proj_lo, of_head(4, 1))
                        query(UPE, 0)
                        query(UPE, 1)
                    head_block(1)
                    eng.wait_ge(pl.proj_lo, of_head(4, 3))
                    if e == 0:
                        eng.wait_ge(pl.rope_lo, L * 10 + p * 2 + 4)
                    for c in range(CC):
                        last = mm3(pe, att[:, 1536 + 64 * c:1536 + 64 * (c + 1)], small_w(UKT, c),
                                   rows_of(q, ALL, slice(NP_, NT)), True, True)
                    last.then_inc(pl.absorbed, 1)
                    half_rows = slice(64 * e, 64 * e + 64)
                    for t in range(KT):
                        tile, keys = slice(P * t, P * (t + 1)), slice(0, P * (t + 1))
                        mm3(pe, score_tile(pl, t), rows_of(q, ALL, tile), rows_of(k_, ALL, keys), True, False)
                        mm3(pe, score_tile(pl, t), rows_of(q_pe, half_rows, tile), rows_of(kpe, half_rows, keys),
                            False, True).then_inc(pl.scored, 1)
                    head_block(2)
                    eng.wait_ge(pl.normed, of_head(4, KT - 1))
                    eng.wait_ge(pl.abs_lo, of_head(1, 0))
                    for j, at in enumerate((1536, 0, 512, 768)):
                        for t in range(j, KT):
                            to = at + P * (t - j)
                            last = pe.transpose(att[:, to:to + P], pl.probs[:, PO[t] + P * j:PO[t] + P * (j + 1)], ident)
                        if j != 2:
                            last.then_inc(pl.turned, 1)
                    head_block(3)
                    eng.wait_ge(pl.turned_lo, of_head(3, 2))
                    for j in range(KT):
                        n = NP_ - P * j
                        last = mm3(pe, att[:, 1024 + P * j:1536], rows_of(v, ALL, slice(P * j, P * (j + 1))),
                                   rows_of(probs_t, ALL, slice(PTO[j], PTO[j] + n)), j == 0, j == KT - 1)
                    last.then_inc(pl.pv_made, 1)
                    head_block(4)

            def wo(m, half, k0=0, k1=KC, ready=None):
                weight = L * NB + (n_wo(m) + 1) if half == 0 and k0 == 0 else None
                block_half(L * RING, (WO_A, WO_B)[half][m], SLOT_WO[m], half, weight, ready, k0, k1)

            def merged_a(k):
                return x_part(L, X_WOA + k)

            def merged_b(k):
                return x_part(L, X_WOS + k // 2)

            def s_scores(t):
                if t == 0:
                    eng.wait_ge(pl.pe_sample, L * 16 + 16)
                    eng.wait_ge(pl.cache_lo, L * 4 + 2)
                    eng.wait_ge(pl.abs_lo, L * HEADS + HEADS)
                else:
                    eng.wait_ge(pl.s_exped, L * 4 + t)
                two = slice(P * t, P * (t + 1))
                for out, latents, rotary, keys in ((att[:, 0:PAST], cache_t, cache_pe, slice(0, PAST)),
                                                   (att[:, PAST:PAST + NS_], ckv, kpe, slice(NP_, NT))):
                    for c in range(CC):
                        mm3(pe, out, rows_of(q_abs, ALL, c, two), rows_of(latents, ALL, c, keys), c == 0, False)
                    last = mm3(pe, out, rows_of(q_pe_sample, slice(0, ROPE), two),
                               rows_of(rotary, slice(0, ROPE), keys), False, True)
                last.then_inc(pl.s_scored, 1)

            def s_turn(t):
                eng.wait_ge(pl.s_normed, L * 4 + t + 1)
                if t == 0:
                    eng.wait_ge(pl.pv_read, L * HEADS + HEADS + 1)
                for j in range(4):
                    pe.transpose(att[:, 1024 + P * j:1024 + P * (j + 1)], pl.ps[:, P * j:P * (j + 1)], ident)
                pe.transpose(att[0:NS_, 576:704], pl.ps[:, PAST:NT], ident).then_inc(pl.s_turned, 1)

            def s_attend(t):
                eng.wait_ge(pl.s_tlo, L * 4 + t + 1)
                if t == 0:
                    eng.wait_ge(pl.cache_lo, L * 4 + 4)
                else:
                    eng.wait_ge(pl.s_merged, L * 4 + t)
                for c in range(CC):
                    for kt in range(5):
                        rows = slice(0, P if kt < 4 else NS_)
                        last = mm3(pe, att[:, 1664 + P * c:1664 + P * (c + 1)],
                                   rows_of(cache_n, rows, kt, slice(P * c, P * (c + 1))),
                                   rows_of(probs_s_t, rows, kt, ALL), kt == 0, kt == 4)
                last.then_inc(pl.s_context, 1)

            def s_values(t):
                eng.wait_ge(pl.s_clo, L * 4 + t + 1)
                eng.wait_ge(pl.small_lo, L * 10 + (9 if t < 2 else 10))
                for hh in range(2):
                    for c in range(CC):
                        at = ((2 * t + hh) % 4 * 2 + c) * P
                        last = mm3(pe, att[:, 1920 + 64 * hh:1920 + 64 * (hh + 1)],
                                   rows_of(small, ALL, slice(at, at + P)),
                                   rows_of(context, ALL, c, slice(64 * hh, 64 * (hh + 1))), c == 0, c == CC - 1)
                last.then_inc(pl.s_valued, 1)

            eng.wait_ge(pl.sample_kept, L + 1)
            eng.sem_inc(pl.waits_apart, 1)
            for c in range(CC):
                last = pe.transpose(att[0:NS_, 1536 + P * c:1536 + P * (c + 1)], pl.kv_sample[:, c, :], ident)
            last.then_inc(pl.new_turned, 1)
            for m in range(4):
                wo(m, 0, 0, 4, merged_a)
            s_scores(0)
            for m in range(4):
                wo(m, 0, 4, KC, merged_a)
            s_turn(0)
            for t in range(2):
                wo(4 + 2 * t, 0)
                s_attend(t)
                s_scores(t + 1)
                wo(5 + 2 * t, 0)
                s_values(t)
                s_turn(t + 1)
            for m in range(2):
                wo(m, 1, 0, 4, merged_b)
            s_attend(2)
            s_scores(3)
            wo(2, 1, 0, 4)
            norm_sum(L, WO_SUM_A, pl.ss[:, 0, :], S_POSTA + 7)
            s_values(2)
            s_turn(3)
            wo(3, 1, 0, 4)
            for m in range(3):
                wo(m, 1, 4, 6, merged_b)
            s_attend(3)
            wo(3, 1, 4, 6)
            s_values(3)
            for m in range(4):
                wo(m, 1, 6, KC, merged_b)
            for m in range(4, KC):
                wo(m, 1)
            norm_sum(L, FF_SUM_A, pl.ss[:, 0, :], S_MIX_O + MIX_O.index((0, KC - 1)))

            def w1_first(half, j):
                weight = L * NB + (n_w1(0, j) + 1) if half == 0 else None
                ready = (lambda k: x_part(L, (X_FFA, X_FFB)[half] + k)) if j == 0 else None
                block_half(L * RING, r_w1(0, half, j), SLOT_W1[j], half, weight, ready)

            def w1(L_ring, L_weight, g):
                for half in range(2):
                    for j in range(4):
                        weight = L_weight + (n_w1(g, j) + 1) if half == 0 else None
                        block_half(L_ring, r_w1(g, half, j), SLOT_W1[j], half, weight)

            def w2_block(free, f_ready, weight, slots, parity, m, half):
                k_ring = 8 * half + m
                eng.wait_ge(pl.w2_free, free + k_ring)
                if m == 0:
                    eng.wait_ge(pl.f_lo, f_ready + 4 * (half + 1))
                if half == 0 and m % 2 == 0:
                    eng.wait_ge(pl.weights_lo, weight + m // 2)
                hi, lo, _ = pl.slot(slots[m // 2])
                out = att[:, 512 * (k_ring % 4):512 * (k_ring % 4) + NH]
                for k in range(4):
                    at = k * 256 + m % 2 * P
                    last = mm3(pe, out, (hi[:, at:at + P], lo[:, at:at + P]), rows_of(f, ALL, parity, k, cols(half)),
                               k == 0, k == 3)
                last.then_inc(pl.w2_full, 1)

            w1_first(0, 0)
            norm_sum(L, WO_SUM_B, pl.ss[:, 1, :], S_MIX_O + MIX_O.index((1, KC - 1)))
            for j in range(1, 4):
                w1_first(0, j)
            w1_first(1, 0)
            norm_sum(L, FF_SUM_B, pl.ss[:, 1, :], S_PREB + 7)
            for j in range(1, 4):
                w1_first(1, j)
            w1(L * RING, L * NB, 1)

            def w2(L_w2, L_f, L_weight, g):
                for half in range(2):
                    for m in range(KC):
                        w2_block(L_w2 + (16 * g + 1), L_f + 8 * g, L_weight + (n_w2(g, 0) + 1), SLOT_W2, g % 2,
                                 m, half)

            w2(L * W2N, L * 64, L * NB, 0)
            with eng.Fori(0, (GROUPS - 2) // 2) as i:
                for e in range(2):
                    w1(L * RING + i * 16, L * NB + i * 16, 2 + e)
                    w2(L * W2N + i * 32, L * 64 + i * 16, L * NB + i * 16, 1 + e)
            g = GROUPS - 1

            def last_w2(m, half):
                w2_block(L * W2N + (16 * g + 1), L * 64 + 8 * g, L * NB + (n_w2(g, 0) + 1), SLOT_W1, g % 2, m, half)

            for m in range(KC):
                last_w2(m, 0)
            last_w2(0, 1)
            norm_sum(L, POST_SUM_A, pl.ss[:, 0, :], S_FPA + 7)
            for m in range(1, KC):
                last_w2(m, 1)
            norm_sum(L, NEXT_SUM_B, pl.ss[:, 1, :], S_MIX_2 + MIX_2.index((1, KC - 1)))


def kernel(x_prompt, x_sample, cache_ckv, cache_kpe, state_conv, w_in, conv_w, w_uq, w_uk, w_uv, w_o, w1, w2,
           g_pre_mix, g_post_mix, g_pre_ffn, g_post_ffn, g_q, g_kv):
    import concourse.bacc as bacc
    from concourse.bass_utils import run_bass_kernel_spmd

    def array(a):
        return np.asarray(a, dtype=np.float32)

    def per_feature(a):
        return a.reshape(a.shape[0] // P, P, *a.shape[1:]).swapaxes(0, 1)

    x = np.concatenate([array(x_prompt)[0], array(x_sample)[0]])
    x_in = per_feature(x.T)

    consts = np.zeros((P, N_CONST), np.float32)
    consts[:, C_ID:C_ID + P] = np.eye(P, dtype=np.float32)
    consts[:, C_ONE:C_ONE + P] = 1.0
    consts[:, C_EPS] = EPS
    for L in range(DEPTH):
        at = C_GAIN + L * NG
        for col, g in ((G_PRE, g_pre_mix), (G_POST, g_post_mix), (G_FF, g_pre_ffn), (G_FPOST, g_post_ffn),
                       (G_Q, g_q), (G_KV, g_kv)):
            a = per_feature(array(g)[L])
            consts[:, at + col:at + col + a.shape[1]] = a
        taps = per_feature(array(conv_w)[L].T)
        consts[:, at + G_CONV:at + G_CONV + 3 * KC] = taps.reshape(P, 3 * KC)
        state = per_feature(array(state_conv)[L, 0].T)
        consts[:, C_STATE + L * 2 * KC:C_STATE + (L + 1) * 2 * KC] = state.reshape(P, 2 * KC)

    inv = (10000.0 ** (-np.arange(0, ROPE, 2) / ROPE)).astype(np.float32)
    angles = np.arange(NT, dtype=np.float32)[None, :] * inv[np.arange(P) % 32][:, None]
    sign = np.where(np.arange(P) // 32 % 2 == 0, -1.0, 1.0).astype(np.float32)[:, None]
    tables = np.stack([np.cos(angles), np.sin(angles) * sign]).astype(np.float32)

    blocks = np.zeros((DEPTH * NB + 1, P, 1024), np.float32)

    def block(n, w):
        blocks[n] = per_feature(w).reshape(P, 1024)

    off_c, off_x, off_q = D, 2 * D, 3 * D
    off_kv = off_q + QL
    off_pe = off_kv + KL
    off_ga = off_pe + ROPE
    off_gb = off_ga + D
    for L in range(DEPTH):
        w, wo, up, down = array(w_in)[L], array(w_o)[L], array(w1)[L], array(w2)[L]
        base = L * NB
        for b in range(QC + CC):
            block(base + b, w[:, off_q + b * P:off_q + (b + 1) * P])
        rotary = w[:, off_pe:off_pe + ROPE]
        block(base + 5, np.concatenate([rotary, rotary], 1))
        for h in range(HEADS):
            for i, off in enumerate((off_gb, off_ga, off_c, off_x, 0)):
                block(base + n_head(h, i), w[:, off + h * P:off + (h + 1) * P])
        for m in range(KC):
            block(base + n_wo(m), wo[:, m * P:(m + 1) * P])
        for g in range(GROUPS):
            for j in range(4):
                block(base + n_w1(g, j), up[:, (4 * g + j) * P:(4 * g + j + 1) * P])
                block(base + n_w2(g, j), down[4 * g * P:4 * (g + 1) * P, j * 256:(j + 1) * 256])

    small = np.zeros((DEPTH * 5, P, SWE + SWO), np.float32)
    uv = np.zeros((DEPTH, P, 1024), np.float32)
    for L in range(DEPTH):
        uq = array(w_uq)[L].reshape(QL, HEADS, QK)
        uk = array(w_uk)[L].reshape(KL, HEADS, NOPE)
        uvs = array(w_uv)[L].reshape(KL, HEADS, P)
        for h in range(HEADS):
            to = small[L * 5 + h // 2][:, SWE * (h % 2):]
            to[:, UQ:UQ + QC * P] = per_feature(uq[:, h, 0:NOPE]).reshape(P, QC * P)
            to[:, UK:UK + CC * P] = per_feature(uk[:, h]).reshape(P, CC * P)
            to[:, UV:UV + CC * P] = per_feature(uvs[:, h]).reshape(P, CC * P)
            to[:, UKT:UKT + KL] = uk[:, h].T
            if h % 2 == 0:
                both = np.concatenate([uq[:, h, NOPE:], uq[:, h + 1, NOPE:]], 1)
                to[:, UPE:UPE + QC * P] = per_feature(both).reshape(P, QC * P)
        values = per_feature(uvs).transpose(0, 2, 1, 3)
        small[L * 5 + 4, :, 0:1024] = values[:, 0:4].reshape(P, 1024)
        uv[L] = values[:, 4:8].reshape(P, 1024)

    ckv, kpe = array(cache_ckv)[:, 0], array(cache_kpe)[:, 0]
    cache_t = ckv.transpose(0, 2, 1).reshape(DEPTH, CC, P, PAST).transpose(0, 2, 1, 3)
    cache_n = ckv.reshape(DEPTH, PAST // P, P, KL).transpose(0, 2, 1, 3)
    cache_pe = kpe.transpose(0, 2, 1)

    nc = bacc.Bacc("TRN2", target_bir_lowering=False, num_devices=1, dynamic_dma_scratch_size=1024)
    arrays, args = {}, []
    for name, a in (("x", x_in), ("consts", consts), ("tables", tables), ("blocks", blocks), ("small", small),
                    ("uv", uv), ("cache_t", cache_t), ("cache_n", cache_n), ("cache_pe", cache_pe)):
        arrays[name + "_in"] = np.ascontiguousarray(a)
        args.append(nc.dram_tensor(name + "_in", a.shape, F32, kind="ExternalInput").ap())
    for name, shape in (("x", (P, KC, NT)), ("kv", (DEPTH, P, CC, NT)), ("kpe", (DEPTH, ROPE, NT)),
                        ("conv", (DEPTH, P, KC, 4))):
        args.append(nc.dram_tensor(name + "_out", shape, F32, kind="ExternalOutput").ap())
    program(nc, *args)
    r = run_bass_kernel_spmd(nc, [arrays], core_ids=[0]).results[0]

    y = r["x_out"].transpose(2, 1, 0).reshape(NT, D)
    kv = r["kv_out"].transpose(0, 3, 2, 1).reshape(DEPTH, 1, NT, KL)
    pe_new = r["kpe_out"].transpose(0, 2, 1)[:, None]
    conv = r["conv_out"].transpose(0, 3, 2, 1).reshape(DEPTH, 1, 4, D)
    return (y[None, 0:NP_], y[None, NP_:], kv[:, :, 0:NP_], pe_new[:, :, 0:NP_], conv[:, :, 0:2],
            kv[:, :, NP_:], pe_new[:, :, NP_:], conv[:, :, 2:4])
```
